# Optimizing a Trainium2 kernel written in Bass

```python
import math
import jax, jax.numpy as jnp
from jax import lax
import numpy as np

D_MODEL = 1024
BATCH = 1
SEQ = 512
DEPTH = 2

GRID_W = 64
CTX_LEN = 256
EPS = 1e-6
ROPE_BASE = 10000.0
HEAD_DIM = 64

SWA_HEADS = 6
SWA_KV_HEADS = 2
SWA_WINDOW = 128
SWA_BLOCK = 128
GDN_HEADS = 6
GDN_DK = 64
GDN_DV = 64
GDN_CONV = 5
GDN_CHUNK = 64
MLA_HEADS = 4
MLA_Q_RANK = 192
MLA_KV_RANK = 128
MLA_NOPE = 64
MLA_ROPE = 32
MLA_V = 64
MLA_BLOCK = 128

D_MIX = SWA_HEADS * HEAD_DIM + GDN_HEADS * GDN_DV + MLA_HEADS * MLA_V
GDN_QKV = 2 * GDN_HEADS * GDN_DK + GDN_HEADS * GDN_DV
PROJ_SPLITS = (SWA_HEADS * HEAD_DIM, SWA_KV_HEADS * HEAD_DIM, SWA_KV_HEADS * HEAD_DIM,
               GDN_QKV, GDN_HEADS * GDN_DV, 4 * GDN_HEADS,
               MLA_Q_RANK, MLA_KV_RANK, MLA_ROPE)
D_PROJ = sum(PROJ_SPLITS)

N_EXPERTS = 64
MOE_TOP_K = 8
MOE_GROUPS = 8
MOE_TOPK_GROUPS = 4
D_EXPERT = 256
D_SHARED = 256
ROUTED_SCALE = 2.5
MOE_BLOCK = 128

kernel_name = "hybrid_dit_hymba_swa_gdn_mla_moe"

def rms_norm(x, gain=None):
    xf = x.astype(jnp.float32)
    y = xf * lax.rsqrt(jnp.mean(xf * xf, axis=-1, keepdims=True) + EPS)
    if gain is not None:
        y = y * gain.astype(jnp.float32)
    return y.astype(x.dtype)

def l2_normalize(t):
    tf = t.astype(jnp.float32)
    return (tf * lax.rsqrt(jnp.sum(tf * tf, axis=-1, keepdims=True) + EPS)).astype(t.dtype)

def grid_positions(n_tokens):
    rows = n_tokens // GRID_W
    row = jnp.repeat(jnp.arange(rows, dtype=jnp.int32), GRID_W)
    col = jnp.tile(jnp.arange(GRID_W, dtype=jnp.int32), rows)
    return row, col

def rope_2d(x, row, col):
    half = x.shape[-1] // 2

    def rot(xh, pos):
        n = xh.shape[-1] // 2
        inv = ROPE_BASE ** (-jnp.arange(n, dtype=jnp.float32) / n)
        ang = pos.astype(jnp.float32)[:, None] * inv[None, :]
        cos, sin = jnp.cos(ang)[:, None, :], jnp.sin(ang)[:, None, :]
        x1, x2 = xh[..., :n], xh[..., n:]
        return jnp.concatenate([x1 * cos - x2 * sin, x1 * sin + x2 * cos], axis=-1)

    return jnp.concatenate([rot(x[..., :half], row), rot(x[..., half:], col)], axis=-1).astype(x.dtype)

def split_proj(p):
    offsets = np.cumsum(PROJ_SPLITS)[:-1].tolist()
    return jnp.split(p, offsets, axis=-1)

def modulation(cvec, w_ada, b_ada):
    return jnp.split(jax.nn.silu(cvec) @ w_ada + b_ada, 6, axis=-1)

def swa_latent(q, k, v, kc, vc, sink):
    B, S, H, d = q.shape
    Bk = SWA_BLOCK
    nb = S // Bk
    G = H // SWA_KV_HEADS
    qb = q.reshape(B, nb, Bk, SWA_KV_HEADS, G, d)

    def neighbours(t):
        tp = jnp.pad(t, ((0, 0), (Bk, Bk), (0, 0), (0, 0))).reshape(B, nb + 2, Bk, SWA_KV_HEADS, d)
        return jnp.concatenate([tp[:, :-2], tp[:, 1:-1], tp[:, 2:]], axis=2)

    kb, vb = neighbours(k), neighbours(v)
    blk = jnp.arange(nb)[:, None, None]
    qpos = blk * Bk + jnp.arange(Bk)[None, :, None]
    kpos = (blk - 1) * Bk + jnp.arange(3 * Bk)[None, None, :]
    valid = (jnp.abs(qpos - kpos) <= SWA_WINDOW) & (kpos >= 0) & (kpos < S)
    scale = d ** -0.5
    s_loc = jnp.einsum('bnqkgd,bnpkd->bnkgqp', qb, kb).astype(jnp.float32) * scale
    s_loc = jnp.where(valid[None, :, None, None], s_loc, -jnp.inf)
    s_ctx = jnp.einsum('bnqkgd,bpkd->bnkgqp', qb, kc).astype(jnp.float32) * scale
    s_sink = jnp.broadcast_to(sink.reshape(SWA_KV_HEADS, G, 1, 1).astype(jnp.float32), s_loc.shape[:-1] + (1,))
    p = jax.nn.softmax(jnp.concatenate([s_loc, s_ctx, s_sink], axis=-1), axis=-1).astype(v.dtype)
    o = (jnp.einsum('bnkgqp,bnpkd->bnqkgd', p[..., :3 * Bk], vb)
         + jnp.einsum('bnkgqp,bpkd->bnqkgd', p[..., 3 * Bk:-1], vc))
    return o.reshape(B, S, H * d)

def swa_context(qc, kc, vc, sink):
    B, L, H, d = qc.shape
    G = H // SWA_KV_HEADS
    qg = qc.reshape(B, L, SWA_KV_HEADS, G, d)
    s = jnp.einsum('bqkgd,bpkd->bkgqp', qg, kc).astype(jnp.float32) * d ** -0.5
    s_sink = jnp.broadcast_to(sink.reshape(SWA_KV_HEADS, G, 1, 1).astype(jnp.float32), s.shape[:-1] + (1,))
    p = jax.nn.softmax(jnp.concatenate([s, s_sink], axis=-1), axis=-1).astype(vc.dtype)
    return jnp.einsum('bkgqp,bpkd->bqkgd', p[..., :-1], vc).reshape(B, L, H * d)

def short_conv(x, w):
    return lax.conv_general_dilated(x, w[:, None, :].astype(x.dtype), window_strides=(1,), padding='SAME',
                                    dimension_numbers=('NWC', 'WIO', 'NWC'), feature_group_count=x.shape[-1])

def gdn_features(qkv, ba, conv_w, a_log, dt_bias):
    B, T, _ = qkv.shape
    qkv = jax.nn.silu(short_conv(qkv, conv_w))
    q, k, v = jnp.split(qkv, [GDN_HEADS * GDN_DK, 2 * GDN_HEADS * GDN_DK], axis=-1)
    q = l2_normalize(q.reshape(B, T, GDN_HEADS, GDN_DK))
    k = l2_normalize(k.reshape(B, T, GDN_HEADS, GDN_DK))
    v = v.reshape(B, T, GDN_HEADS, GDN_DV)
    baf = ba.astype(jnp.float32)
    beta = jax.nn.sigmoid(baf[..., :2 * GDN_HEADS]).reshape(B, T, 2, GDN_HEADS)
    a = baf[..., 2 * GDN_HEADS:].reshape(B, T, 2, GDN_HEADS)
    g = -jnp.exp(a_log.astype(jnp.float32)) * jax.nn.softplus(a + dt_bias.astype(jnp.float32))
    return q, k, v, beta, g

def gated_delta_chunked(q, k, v, g, beta, state0, with_output):
    B, T, H, dk = q.shape
    dv = v.shape[-1]
    out_dtype = v.dtype
    C = GDN_CHUNK
    n = T // C
    f32 = jnp.float32

    def to_chunks(t):
        return jnp.moveaxis(t.astype(f32).reshape((B, n, C, H) + t.shape[3:]), 3, 1)

    q, k, v, g, beta = map(to_chunks, (q, k, v, g, beta))
    gc = jnp.cumsum(g, axis=-1)
    incl = jnp.tril(jnp.ones((C, C), dtype=bool))
    strict = jnp.tril(jnp.ones((C, C), dtype=bool), -1)
    decay = jnp.exp(jnp.where(incl, gc[..., :, None] - gc[..., None, :], -jnp.inf))
    k_beta = k * beta[..., None]
    lower = jnp.where(strict, jnp.einsum('bhnid,bhnjd->bhnij', k_beta, k) * decay, 0.0)
    rhs = jnp.concatenate([v * beta[..., None], k_beta * jnp.exp(gc)[..., None]], axis=-1)
    sol = lax.linalg.triangular_solve(jnp.eye(C, dtype=f32) + lower, rhs,
                                      left_side=True, lower=True, unit_diagonal=True)
    u, w = sol[..., :dv], sol[..., dv:]
    k_out = k * jnp.exp(gc[..., -1:] - gc)[..., None]
    g_tot = jnp.exp(gc[..., -1])
    chunk_major = lambda t: jnp.moveaxis(t, 2, 0)
    if with_output:
        qs = q * dk ** -0.5
        intra = jnp.where(incl, jnp.einsum('bhnid,bhnjd->bhnij', qs, k) * decay, 0.0)
        xs = tuple(map(chunk_major, (u, w, k_out, g_tot, qs * jnp.exp(gc)[..., None], intra)))
    else:
        xs = tuple(map(chunk_major, (u, w, k_out, g_tot)))

    def step(S, inp):
        u_i, w_i, k_i, gt_i = inp[:4]
        v_new = u_i - jnp.einsum('bhcd,bhde->bhce', w_i, S)
        S_next = S * gt_i[..., None, None] + jnp.einsum('bhcd,bhce->bhde', k_i, v_new)
        if not with_output:
            return S_next, None
        q_i, a_i = inp[4:]
        o_i = jnp.einsum('bhcd,bhde->bhce', q_i, S) + jnp.einsum('bhij,bhje->bhie', a_i, v_new)
        return S_next, o_i

    S_final, o = lax.scan(step, state0.astype(f32), xs)
    if not with_output:
        return None, S_final
    o = jnp.moveaxis(jnp.moveaxis(o, 0, 2), 1, 3).reshape(B, T, H, dv)
    return o.astype(out_dtype), S_final

def gdn_bidirectional(lat, ctx, ctx_out):
    qL, kL, vL, bL, gL = lat
    qC, kC, vC, bC, gC = ctx
    rev = lambda t: jnp.flip(t, axis=1)
    S0 = jnp.zeros((qL.shape[0], GDN_HEADS, GDN_DK, GDN_DV), jnp.float32)
    oCf, SCf = gated_delta_chunked(qC, kC, vC, gC[:, :, 0], bC[:, :, 0], S0, ctx_out)
    oLf, _ = gated_delta_chunked(qL, kL, vL, gL[:, :, 0], bL[:, :, 0], SCf, True)
    oCb, SCb = gated_delta_chunked(rev(qC), rev(kC), rev(vC), rev(gC[:, :, 1]), rev(bC[:, :, 1]), S0, ctx_out)
    oLb, _ = gated_delta_chunked(rev(qL), rev(kL), rev(vL), rev(gL[:, :, 1]), rev(bL[:, :, 1]), SCb, True)
    o_lat = oLf + rev(oLb)
    o_ctx = oCf + rev(oCb) if ctx_out else None
    return o_lat, o_ctx

def gdn_output(o, z, norm_w):
    B, T = o.shape[:2]
    z = z.reshape(B, T, GDN_HEADS, GDN_DV)
    return (rms_norm(o, norm_w) * jax.nn.silu(z)).reshape(B, T, GDN_HEADS * GDN_DV)

def mla_queries(cq, q_norm, w_uq, row, col):
    B, T = cq.shape[:2]
    q = (rms_norm(cq, q_norm) @ w_uq).reshape(B, T, MLA_HEADS, MLA_NOPE + MLA_ROPE)
    qn, qr = q[..., :MLA_NOPE], q[..., MLA_NOPE:]
    if row is not None:
        qr = rope_2d(qr, row, col)
    return qn, qr

def mla_keys(ckv, kr, kv_norm, w_ukv, row, col):
    B, T = ckv.shape[:2]
    kv = (rms_norm(ckv, kv_norm) @ w_ukv).reshape(B, T, MLA_HEADS, MLA_NOPE + MLA_V)
    kn, v = kv[..., :MLA_NOPE], kv[..., MLA_NOPE:]
    if row is not None:
        kr = rope_2d(kr[:, :, None, :], row, col)[:, :, 0]
    return kn, kr, v

def mla_attend(qn, qr, kn, kr, v):
    s = jnp.einsum('bqhd,bkhd->bhqk', qn, kn) + jnp.einsum('bqhr,bkr->bhqk', qr, kr)
    p = jax.nn.softmax(s.astype(jnp.float32) * (MLA_NOPE + MLA_ROPE) ** -0.5, axis=-1).astype(v.dtype)
    return jnp.einsum('bhqk,bkhd->bqhd', p, v)

def mla_latent(qn, qr, kn, kr, v):
    B, S = qn.shape[:2]
    nb = S // MLA_BLOCK

    def blocks(t):
        return jnp.moveaxis(t.reshape((B, nb, MLA_BLOCK) + t.shape[2:]), 1, 0)

    o = lax.map(lambda qs: mla_attend(qs[0], qs[1], kn, kr, v), (blocks(qn), blocks(qr)))
    return jnp.moveaxis(o, 0, 1).reshape(B, S, MLA_HEADS * MLA_V)

def token_mixer(h, hc, w_in, w_out, swa_sink, conv_w, a_log, dt_bias, gdn_norm_w,
                q_norm, w_uq, kv_norm, w_ukv, row, col, ctx_out):
    B, S, _ = h.shape
    L = hc.shape[1]
    pl = split_proj(h @ w_in)
    pc = split_proj(hc @ w_in)
    qa = rope_2d(pl[0].reshape(B, S, SWA_HEADS, HEAD_DIM), row, col)
    ka = rope_2d(pl[1].reshape(B, S, SWA_KV_HEADS, HEAD_DIM), row, col)
    va = pl[2].reshape(B, S, SWA_KV_HEADS, HEAD_DIM)
    kca = pc[1].reshape(B, L, SWA_KV_HEADS, HEAD_DIM)
    vca = pc[2].reshape(B, L, SWA_KV_HEADS, HEAD_DIM)
    oa = swa_latent(qa, ka, va, kca, vca, swa_sink)
    featL = gdn_features(pl[3], pl[5], conv_w, a_log, dt_bias)
    featC = gdn_features(pc[3], pc[5], conv_w, a_log, dt_bias)
    obL, obC = gdn_bidirectional(featL, featC, ctx_out)
    ob = gdn_output(obL, pl[4], gdn_norm_w)
    qnL, qrL = mla_queries(pl[6], q_norm, w_uq, row, col)
    knL, krL, vL = mla_keys(pl[7], pl[8], kv_norm, w_ukv, row, col)
    knC, krC, vC = mla_keys(pc[7], pc[8], kv_norm, w_ukv, None, None)
    oc = mla_latent(qnL, qrL, jnp.concatenate([knL, knC], axis=1), jnp.concatenate([krL, krC], axis=1),
                    jnp.concatenate([vL, vC], axis=1))
    y = jnp.concatenate([oa, ob, oc], axis=-1) @ w_out
    if not ctx_out:
        return y, None
    oca = swa_context(pc[0].reshape(B, L, SWA_HEADS, HEAD_DIM), kca, vca, swa_sink)
    obc = gdn_output(obC, pc[4], gdn_norm_w)
    qnC, qrC = mla_queries(pc[6], q_norm, w_uq, None, None)
    occ = mla_attend(qnC, qrC, knC, krC, vC).reshape(B, L, MLA_HEADS * MLA_V)
    yc = jnp.concatenate([oca, obc, occ], axis=-1) @ w_out
    return y, yc

def swiglu(t, wg, wu, wd):
    return (jax.nn.silu(t @ wg) * (t @ wu)) @ wd

def route(h, router_w, router_bias):
    N = h.shape[0]
    scores = jax.nn.sigmoid((h @ router_w).astype(jnp.float32))
    sel = scores + router_bias.astype(jnp.float32)
    grouped = sel.reshape(N, MOE_GROUPS, N_EXPERTS // MOE_GROUPS)
    group_score = lax.top_k(grouped, 2)[0].sum(-1)
    _, top_groups = lax.top_k(group_score, MOE_TOPK_GROUPS)
    group_mask = jnp.any(top_groups[:, :, None] == jnp.arange(MOE_GROUPS)[None, None, :], axis=1)
    masked = jnp.where(jnp.repeat(group_mask, N_EXPERTS // MOE_GROUPS, axis=1), sel, -jnp.inf)
    _, top_idx = lax.top_k(masked, MOE_TOP_K)
    w = jnp.take_along_axis(scores, top_idx, axis=1)
    return top_idx, w / jnp.sum(w, axis=-1, keepdims=True) * ROUTED_SCALE

def moe_ffn(h, router_w, router_bias, w_gate, w_up, w_down, s_gate, s_up, s_down):
    N, D = h.shape
    top_idx, top_w = route(h, router_w, router_bias)
    NK = N * MOE_TOP_K
    e = top_idx.reshape(-1)
    tok = jnp.arange(NK, dtype=jnp.int32) // MOE_TOP_K
    wts = top_w.reshape(-1).astype(h.dtype)
    order = jnp.argsort(e)
    e_s = e[order]
    counts = jnp.bincount(e, length=N_EXPERTS)
    starts = jnp.cumsum(counts) - counts
    pcounts = (counts + MOE_BLOCK - 1) // MOE_BLOCK * MOE_BLOCK
    pends = jnp.cumsum(pcounts)
    dest = (pends - pcounts)[e_s] + jnp.arange(NK, dtype=jnp.int32) - starts[e_s]
    n_blocks = -(-NK // MOE_BLOCK) + N_EXPERTS
    P = n_blocks * MOE_BLOCK
    buf_tok = jnp.full((P,), N, jnp.int32).at[dest].set(tok[order])
    buf_w = jnp.zeros((P,), h.dtype).at[dest].set(wts[order])
    blk_exp = jnp.minimum(jnp.searchsorted(pends, jnp.arange(n_blocks) * MOE_BLOCK, side='right'), N_EXPERTS - 1)
    xb = jnp.concatenate([h, jnp.zeros((1, D), h.dtype)], axis=0)[buf_tok].reshape(n_blocks, MOE_BLOCK, D)
    yb = lax.map(lambda a: swiglu(a[0], w_gate[a[1]], w_up[a[1]], w_down[a[1]]), (xb, blk_exp))
    yb = yb.reshape(P, D) * buf_w[:, None]
    routed = jnp.zeros((N + 1, D), yb.dtype).at[buf_tok].add(yb)[:N]
    return swiglu(h, s_gate, s_up, s_down) + routed

def setup_inputs(seed: int = 0) -> dict:
    key = jax.random.key(seed)
    ks = iter(jax.random.split(key, 40))
    nrm = lambda shape, scale: scale * jax.random.normal(next(ks), shape, jnp.float32)
    gain = lambda shape: 1.0 + nrm(shape, 0.02)
    dt = jnp.exp(jax.random.uniform(next(ks), (DEPTH, 2, GDN_HEADS), jnp.float32,
                                    minval=math.log(1e-3), maxval=math.log(1e-1)))
    return {
        "x": nrm((BATCH, SEQ, D_MODEL), 1.0),
        "c": nrm((BATCH, D_MODEL), 1.0),
        "ctx": nrm((BATCH, CTX_LEN, D_MODEL), 1.0),
        "c_ctx": nrm((D_MODEL,), 1.0),
        "ada_w": nrm((DEPTH, D_MODEL, 6 * D_MODEL), 0.5 * D_MODEL ** -0.5),
        "ada_b": nrm((DEPTH, 6 * D_MODEL), 0.02),
        "mix_norm_pre": gain((DEPTH, D_MODEL)),
        "mix_norm_post": gain((DEPTH, D_MODEL)),
        "ffn_norm_pre": gain((DEPTH, D_MODEL)),
        "ffn_norm_post": gain((DEPTH, D_MODEL)),
        "w_in": nrm((DEPTH, D_MODEL, D_PROJ), D_MODEL ** -0.5),
        "w_out": nrm((DEPTH, D_MIX, D_MODEL), D_MIX ** -0.5),
        "swa_sink": nrm((DEPTH, SWA_HEADS), 0.5),
        "gdn_conv_w": nrm((DEPTH, GDN_CONV, GDN_QKV), GDN_CONV ** -0.5),
        "gdn_a_log": jnp.log(jax.random.uniform(next(ks), (DEPTH, 2, GDN_HEADS), jnp.float32, minval=1.0, maxval=16.0)),
        "gdn_dt_bias": dt + jnp.log(-jnp.expm1(-dt)),
        "gdn_norm_w": gain((DEPTH, GDN_DV)),
        "mla_q_norm": gain((DEPTH, MLA_Q_RANK)),
        "mla_w_uq": nrm((DEPTH, MLA_Q_RANK, MLA_HEADS * (MLA_NOPE + MLA_ROPE)), MLA_Q_RANK ** -0.5),
        "mla_kv_norm": gain((DEPTH, MLA_KV_RANK)),
        "mla_w_ukv": nrm((DEPTH, MLA_KV_RANK, MLA_HEADS * (MLA_NOPE + MLA_V)), MLA_KV_RANK ** -0.5),
        "router_w": nrm((DEPTH, D_MODEL, N_EXPERTS), D_MODEL ** -0.5),
        "router_bias": nrm((DEPTH, N_EXPERTS), 0.01),
        "expert_w_gate": nrm((DEPTH, N_EXPERTS, D_MODEL, D_EXPERT), D_MODEL ** -0.5),
        "expert_w_up": nrm((DEPTH, N_EXPERTS, D_MODEL, D_EXPERT), D_MODEL ** -0.5),
        "expert_w_down": nrm((DEPTH, N_EXPERTS, D_EXPERT, D_MODEL), D_EXPERT ** -0.5),
        "shared_w_gate": nrm((DEPTH, D_MODEL, D_SHARED), D_MODEL ** -0.5),
        "shared_w_up": nrm((DEPTH, D_MODEL, D_SHARED), D_MODEL ** -0.5),
        "shared_w_down": nrm((DEPTH, D_SHARED, D_MODEL), D_SHARED ** -0.5),
    }

def reference(x, c, ctx, c_ctx, ada_w, ada_b, mix_norm_pre, mix_norm_post, ffn_norm_pre, ffn_norm_post,
              w_in, w_out, swa_sink, gdn_conv_w, gdn_a_log, gdn_dt_bias, gdn_norm_w,
              mla_q_norm, mla_w_uq, mla_kv_norm, mla_w_ukv, router_w, router_bias,
              expert_w_gate, expert_w_up, expert_w_down, shared_w_gate, shared_w_up, shared_w_down):
    B, S, D = x.shape
    L = ctx.shape[1]
    row, col = grid_positions(S)
    for layer in range(DEPTH):
        last = layer == DEPTH - 1
        sh1, sc1, g1, sh2, sc2, g2 = [t[:, None, :] for t in modulation(c, ada_w[layer], ada_b[layer])]
        csh1, csc1, cg1, csh2, csc2, cg2 = modulation(c_ctx, ada_w[layer], ada_b[layer])
        h = rms_norm(x, mix_norm_pre[layer]) * (1.0 + sc1) + sh1
        hc = rms_norm(ctx, mix_norm_pre[layer]) * (1.0 + csc1) + csh1
        y, yc = token_mixer(h, hc, w_in[layer], w_out[layer], swa_sink[layer], gdn_conv_w[layer],
                            gdn_a_log[layer], gdn_dt_bias[layer], gdn_norm_w[layer], mla_q_norm[layer],
                            mla_w_uq[layer], mla_kv_norm[layer], mla_w_ukv[layer], row, col, not last)
        x = x + g1 * rms_norm(y, mix_norm_post[layer])
        moe_args = (router_w[layer], router_bias[layer], expert_w_gate[layer], expert_w_up[layer],
                    expert_w_down[layer], shared_w_gate[layer], shared_w_up[layer], shared_w_down[layer])
        h2 = rms_norm(x, ffn_norm_pre[layer]) * (1.0 + sc2) + sh2
        if last:
            f = moe_ffn(h2.reshape(B * S, D), *moe_args).reshape(B, S, D)
        else:
            ctx = ctx + cg1 * rms_norm(yc, mix_norm_post[layer])
            h2c = rms_norm(ctx, ffn_norm_pre[layer]) * (1.0 + csc2) + csh2
            f_all = moe_ffn(jnp.concatenate([h2.reshape(B * S, D), h2c.reshape(B * L, D)], axis=0), *moe_args)
            f, fc = f_all[:B * S].reshape(B, S, D), f_all[B * S:].reshape(B, L, D)
            ctx = ctx + cg2 * rms_norm(fc, ffn_norm_post[layer])
        x = x + g2 * rms_norm(f, ffn_norm_post[layer])
    return x


_drawn_inputs = setup_inputs


def setup_inputs(seed=0):
    import zlib

    import numpy as np

    out = dict(_drawn_inputs(seed))
    spreads = {}
    factors = {'ffn_norm_post': 3.424, 'swa_sink': 8.0, 'mla_q_norm': 7.126, 'mla_kv_norm': 3.315}
    for name, (base, spread) in spreads.items():
        noise = np.random.default_rng([zlib.crc32(name.encode()), seed]).standard_normal(out[name].shape)
        drawn = base * np.exp(spread * noise) if base else spread * noise
        out[name] = __import__('jax').numpy.asarray(drawn.astype(out[name].dtype))
    for name, factor in factors.items():
        out[name] = (out[name] * factor).astype(out[name].dtype)
    return out
```

```python
import numpy as np
import concourse.bass as bass
from concourse import mybir
from contextlib import ExitStack

F32 = mybir.dt.float32
I32 = mybir.dt.int32
ACT = mybir.ActivationFunctionType
ALU = mybir.AluOpType
AX = mybir.AxisListType

P = 128
D = 1024
DK = D // P
NLAYER = 2
SEQ, CTXN = 512, 256
NLT, NT = SEQ // P, (SEQ + CTXN) // P
NTOK = NT * P
EPS = 1e-6
GRID_W = 64
SWA_H, SWA_KV, HD = 6, 2, 64
GH = 6
MH, MNOPE, MROPE = 4, 64, 32
MQ = MNOPE + MROPE
QR, KVR = 192, 128
W_ATT = SWA_H * HD + 2 * SWA_KV * HD + QR + KVR + MROPE
O_K, O_V = SWA_H * HD, SWA_H * HD + SWA_KV * HD
O_CQ = O_V + SWA_KV * HD
O_CKV = O_CQ + QR
O_KR = O_CKV + KVR
W_ZB = GH * HD + 4 * GH
W_TOK = W_ATT + W_ZB
GCH = 3 * GH * HD
NGT = GCH // P
CONV = 5
PAD = CONV // 2
CW = PAD + SEQ + 2 * PAD + CTXN + PAD
CTX0 = PAD + SEQ + 2 * PAD
CHUNK = 64
NLEV = 6
NE, TOPK, DE = 64, 8, 256
NGRP, GSZ, TOPG = 8, 8, 4
ROUTED_SCALE = 2.5
BIG = 1e30


def tile_col(i):
    return PAD + i * P if i < NLT else CTX0 + (i - NLT) * P


def shape_constants():
    parts, at, n = {}, {}, 0
    i = np.arange(P)
    same = (i[:, None] // CHUNK) == (i[None, :] // CHUNK)
    parts["ident"] = np.eye(P)
    parts["ones"] = np.ones((P, P))
    parts["tri"] = np.concatenate([same & (i[:, None] <= i[None, :]), same & (i[:, None] >= i[None, :])], 1)
    parts["chunk"] = same
    parts["half"] = np.concatenate([np.repeat((i[:, None] // CHUNK) == r, P, 1) for r in range(2)], 1)
    lev = []
    for d in range(2):
        for v in range(NLEV):
            s = 1 << v
            blk = (i[:, None] // (2 * s)) == (i[None, :] // (2 * s))
            late, early = (i // s) % 2 == 1 - d, (i // s) % 2 == d
            lev.append(blk & late[:, None] & early[None, :])
    parts["level"] = np.concatenate(lev, 1)
    parts["before"] = i[:, None] < i[None, :]
    parts["prev"] = np.where(i[None, :] >= i[:, None], 0.0, -BIG)
    parts["next"] = np.where(i[None, :] <= i[:, None], 0.0, -BIG)

    def rope(dim):
        half = dim // 2
        n = half // 2
        inv = (np.float32(10000.0) ** (-np.arange(n, dtype=np.float32) / np.float32(n))).astype(np.float32)
        cos, sin = np.ones((NTOK, dim)), np.zeros((NTOK, dim))
        t = np.arange(SEQ)
        for k, pos in enumerate((t // GRID_W, t % GRID_W)):
            ang = (pos.astype(np.float32)[:, None] * inv[None, :]).astype(np.float32).astype(np.float64)
            for s in range(2):
                c = k * half + s * n
                cos[:SEQ, c:c + n] = np.cos(ang)
                sin[:SEQ, c:c + n] = np.sin(ang) * (-1 if s == 0 else 1)
        lay = lambda a: a.reshape(NT, P, dim).transpose(1, 0, 2).reshape(P, NT * dim)
        return np.concatenate([lay(cos), lay(sin)], 1)

    parts["rope_swa"] = rope(HD)
    parts["rope_mla"] = rope(MROPE)
    parts["gcmp"] = np.tile((np.arange(NGRP)[None, :] < np.arange(NGRP)[:, None]).reshape(1, -1), (P, 1))
    parts["tokid"] = i[:, None] + P * np.arange(NT)[None, :]
    parts["iota"] = np.tile(np.arange(P)[None, :], (P, 1))
    for k, v in parts.items():
        at[k] = (n, n + v.shape[1])
        n += v.shape[1]
    return np.ascontiguousarray(np.concatenate([np.asarray(v, np.float64) for v in parts.values()], 1)
                                .astype(np.float32)), at


COLS = [("mix_pre", DK), ("mix_post", DK), ("ffn_pre", DK), ("ffn_post", DK), ("ada_b", 6 * DK), ("conv", NGT * CONV)]
ROWS = [("sink", SWA_H), ("a_log", 2 * GH), ("dt_bias", 2 * GH), ("gdn_norm", HD), ("q_norm", QR),
        ("kv_norm", KVR), ("router_bias", NE)]


def small_layout():
    at, n = {}, 0
    for k, w in COLS + ROWS:
        at[k] = (n, n + w)
        n += w
    return at, n


class Chain:

    def __init__(self, eng, sem):
        self.eng, self.sem, self.n = eng, sem, 0

    def __call__(self, ins):
        ins.then_inc(self.sem, 1)
        self.n += 1
        self.eng.wait_ge(self.sem, self.n)


class Sems:

    def __init__(self, nc, tag):
        self.nc, self.tag, self.all = nc, tag, []

    def __call__(self, name):
        s = self.nc.alloc_semaphore(f"{self.tag}_{name}")
        self.all.append(s)
        return s

    def end(self):
        self.nc.clear_and_free_semaphores(self.all)
        self.nc.all_engine_barrier()


class Arena:

    def __init__(self, tensor, words):
        self.tensor, self.words, self.used = tensor, words, []

    def take(self, stack, name, shape, dt=F32):
        n = int(np.prod(shape[1:]))
        n += n % 2
        at = 0
        for a, b in sorted(self.used):
            if a - at >= n:
                break
            at = max(at, b)
        assert at + n <= self.words, f"no room for {name}: {n} words, at {at} of {self.words}"
        span = (at, at + n)
        self.used.append(span)
        stack.callback(self.used.remove, span)
        ap = self.tensor[0:shape[0], at:at + int(np.prod(shape[1:]))]
        if dt != F32:
            ap = ap.bitcast(dt)
        if len(shape) > 2:
            names = [f"d{k}" for k in range(len(shape) - 1)]
            ap = ap.rearrange(f"p ({' '.join(names)}) -> p {' '.join(names)}", **dict(zip(names[1:], shape[2:])))
        return ap


ARENA_WORDS = 53200


def build(nc, A, out):
    C_AT = shape_constants()[1]
    S_AT, NSMALL = small_layout()
    NCONST = max(b for _, b in C_AT.values())
    dram = lambda name, shape, dt=F32: nc.dram_tensor(name, shape, dt).ap()
    xres = dram("xres", (NTOK, D))
    h2_dram = dram("h2", (NTOK, D))
    cat_dram = dram("cat", (NTOK, D))
    NBMAX = NT + NT * TOPK + NE
    y_dram = dram("y_slots", (NBMAX * P, D))

    outer = ExitStack()
    with outer:
        arena = Arena(outer.enter_context(nc.sbuf_tensor("arena", [P, ARENA_WORDS], F32)), ARENA_WORDS)
        sbuf = arena.take
        psum = outer.enter_context(nc.psum_tensor("psum", [P, 8, 512], F32))
        const = sbuf(outer, "const", [P, NCONST])
        small = sbuf(outer, "small", [P, NLAYER, NSMALL])
        mod = sbuf(outer, "mod", [P, NLAYER, 6 * DK, 2])

        def cst(name, a=0, b=None):
            lo, hi = C_AT[name]
            return const[:, lo + a:(lo + b if b is not None else hi)]

        def par(l, name, a=0, b=None):
            lo, hi = S_AT[name]
            return small[:, l, lo + a:(lo + b if b is not None else hi)]

        def phase_modulation():
            NB = NLAYER * 12
            RING = 4
            st, S = ExitStack(), Sems(nc, "mod")
            with st:
                wa = sbuf(st, "wa", [P, RING, DK, 512])
                row = sbuf(st, "row", [2, RING, 512])
                cc = sbuf(st, "cc", [P, DK, 2])
                sc = sbuf(st, "sc", [P, DK, 2])
                consts_in, cond_in, silu_done, copied = S("consts_in"), S("cond_in"), S("silu_done"), S("copied")
                w_in = [S(f"w_in{r}") for r in range(RING)]
                prod, row_ready, turned, bias_added = S("prod"), S("row_ready"), S("turned"), S("bias_added")
                with nc.Block() as block:
                    @block.sync
                    def _(sp):
                        sp.dma_start(cc[:, :, :], A["cond"]).then_inc(cond_in, 16)
                        sp.dma_start(small[:, :, :], A["small"].rearrange("l p n -> p l n")).then_inc(consts_in, 16)
                        sp.dma_start(const[:, :], A["const"]).then_inc(consts_in, 16)
                        for r in range(RING):
                            sp.dma_start(wa[:, r], A["ada"][r]).then_inc(w_in[r], 16)
                        with sp.Fori(1, NB // RING) as i:
                            for r in range(RING):
                                sp.wait_ge(prod, RING * (i - 1) + r + 1)
                                sp.dma_start(wa[:, r].rearrange("p k n -> p (k n)"),
                                             A["ada"][bass.ds(RING * i + r, 1)].rearrange("b p k n -> (b p) (k n)")
                                             ).then_inc(w_in[r], 16)
                        sp.dma_start(xres[0:SEQ, :], A["x"]).then_inc(consts_in, 16)
                        sp.dma_start(xres[SEQ:NTOK, :], A["ctx"]).then_inc(consts_in, 16)
                        sp.wait_ge(consts_in, 64)

                    @block.scalar
                    def _(act):
                        act.wait_ge(cond_in, 16)
                        nc.scalar.activation(sc[:, :, :], cc[:, :, :], ACT.Silu).then_inc(silu_done, 1)
                        with act.Fori(0, NB // RING) as i:
                            for r in range(RING):
                                act.wait_ge(prod, RING * i + r + 1)
                                nc.scalar.copy(row[:, r], psum[0:2, r, :]).then_inc(row_ready, 1)

                    @block.tensor
                    def _(pe):
                        pe.wait_ge(silu_done, 1)
                        pe.wait_ge(consts_in, 32)
                        with pe.Fori(0, NB // RING) as i:

                            def turn(r):
                                pe.wait_ge(row_ready, RING * i + r + 1)
                                pe.wait_ge(copied, RING * i + r + 1)
                                for n in range(4):
                                    last = nc.tensor.matmul(psum[:, RING + r, 2 * n:2 * n + 2], row[:, r, n * P:(n + 1) * P],
                                                            cst("ident", 0, 2)[0:2], start=True, stop=True)
                                last.then_inc(turned, 1)

                            for r in range(RING):
                                pe.wait_ge(w_in[r], 16 * i + 16)
                                for k in range(DK):
                                    last = nc.tensor.matmul(psum[0:2, r, :], sc[:, k, :], wa[:, r, k, :],
                                                            start=(k == 0), stop=(k == DK - 1))
                                last.then_inc(prod, 1)
                                if r:
                                    turn(r - 1)
                            turn(RING - 1)

                    @block.vector
                    def _(dve):
                        for r in range(RING):
                            nc.vector.memset(psum[:, RING + r, 0:8], 0.0).then_inc(copied, 1)
                        flat = mod[:, :, :, :].rearrange("p l n s -> p (l n s)")
                        with dve.Fori(0, NB // RING) as i:
                            for r in range(RING):
                                dve.wait_ge(turned, RING * i + r + 1)
                                nc.vector.tensor_copy(flat[:, bass.ds(8 * RING * i + 8 * r, 8)],
                                                      psum[:, RING + r, 0:8]).then_inc(copied, 1)
                        dve.wait_ge(consts_in, 32)
                        dve.wait_ge(copied, RING + NB)
                        for l in range(NLAYER):
                            nc.vector.tensor_tensor(mod[:, l], mod[:, l],
                                                    par(l, "ada_b").unsqueeze(2).to_broadcast([P, 6 * DK, 2]),
                                                    ALU.add).then_inc(bias_added, 1)
                S.end()

        def make_rows(l, tag, kinds, rows):
            st, S = ExitStack(), Sems(nc, f"rows{tag}{l}")
            n_items = 2 * len(kinds)
            with st:
                col = sbuf(st, "col", [P, len(kinds), 2, DK])
                diag = sbuf(st, "diag", [P, 2, D])
                step, diag_ready, bcast, copied = S("step"), S("diag_ready"), S("bcast"), S("copied")
                with nc.Block() as block:
                    @block.vector
                    def _(dve):
                        ch = Chain(dve, step)
                        for j, (slot, gain, plus) in enumerate(kinds):
                            src = mod[:, l, slot * DK:(slot + 1) * DK, :].rearrange("p k s -> p s k")
                            g = par(l, gain).unsqueeze(1).to_broadcast([P, 2, DK]) if gain else None
                            if gain is None:
                                ch(nc.vector.tensor_copy(col[:, j], src))
                            elif plus:
                                ch(nc.vector.scalar_tensor_tensor(out=col[:, j], in0=src, scalar=1.0, in1=g,
                                                                  op0=ALU.add, op1=ALU.mult))
                            else:
                                ch(nc.vector.tensor_tensor(col[:, j], src, g, ALU.mult))
                        for n in range(n_items):
                            if n >= 2:
                                dve.wait_ge(bcast, n - 1)
                            nc.vector.tensor_tensor(
                                diag[:, n % 2].rearrange("p (k c) -> p k c", c=P),
                                cst("ident").unsqueeze(1).to_broadcast([P, DK, P]),
                                col[:, n // 2, n % 2].unsqueeze(2).to_broadcast([P, DK, P]), ALU.mult).then_inc(diag_ready, 1)

                    @block.tensor
                    def _(pe):
                        for n in range(n_items):
                            pe.wait_ge(diag_ready, n + 1)
                            if n >= 2:
                                pe.wait_ge(copied, n - 1)
                            for c in range(2):
                                last = nc.tensor.matmul(psum[:, 2 * (n % 2) + c, :], cst("ones"),
                                                        diag[:, n % 2, c * 512:(c + 1) * 512], start=True, stop=True)
                            last.then_inc(bcast, 1)

                    @block.scalar
                    def _(act):
                        for n in range(n_items):
                            act.wait_ge(bcast, n + 1)
                            nc.scalar.copy(rows[:, n // 2, n % 2, :].rearrange("p (c n) -> p c n", c=2),
                                           psum[:, 2 * (n % 2):2 * (n % 2) + 2, :]).then_inc(copied, 1)
                S.end()

        def phase_project(l, patt, pzb, chan):
            TOKC = [(0, 512), (512, W_ATT), (W_ATT, W_TOK)]
            GC = 3
            RING = 3
            st, S = ExitStack(), Sems(nc, f"proj{l}")
            with st:
                rows = sbuf(st, "rows1", [P, 2, 2, D])
                make_rows(l, "a", [(1, "mix_pre", True), (0, None, False)], rows)
                wt = sbuf(st, "wt", [P, RING, DK, 512])
                xt = sbuf(st, "xt", [P, 2, D])
                sq = sbuf(st, "sq", [P, D])
                hh = sbuf(st, "hh", [P, 2, D])
                hT = sbuf(st, "hT", [P, DK, NTOK])
                ss = sbuf(st, "ss", [P, NT])
                rs = sbuf(st, "rs", [P, NT])
                mh = sbuf(st, "mh", [P, 1])
                x_in, w_in, sq_done, ms_done = [S("x_in0"), S("x_in1")], [S(f"w_in{r}") for r in range(RING)], S("sq_done"), S("ms_done")
                rstd, step, h_ready, turned, hT_ready = S("rstd"), S("step"), S("h_ready"), S("turned"), S("hT_ready")
                prod, out_v, out_s, ch_zero = S("prod"), S("out_v"), S("out_s"), S("ch_zero")
                NCH = len(TOKC) + GC
                items = []
                for c, (a, b) in enumerate(TOKC):
                    for i in range(NT):
                        items.append((c, "tok", i, a, b))
                for c in range(GC):
                    for j in range(3):
                        for s in range(2):
                            items.append((len(TOKC) + c, "chan", 3 * c + j, s, j))
                last_of = {}
                for n, it in enumerate(items):
                    last_of[it[0]] = n

                def dest(it):
                    _, kind, i, a, b = it
                    if kind == "tok":
                        return patt[:, i, a:b] if b <= W_ATT else pzb[:, i, 0:W_ZB]
                    return chan[:, i, PAD:PAD + SEQ] if a == 0 else chan[:, i, CTX0:CTX0 + CTXN]

                def width(it):
                    _, kind, i, a, b = it
                    return b - a if kind == "tok" else (SEQ, CTXN)[a]

                with nc.Block() as block:
                    @block.sync
                    def _(sp):
                        def load_w(c):
                            r = c % RING
                            if c >= RING:
                                sp.wait_ge(prod, last_of[c - RING] + 1)
                            if c < len(TOKC):
                                a, b = TOKC[c]
                                src, w = A["w_tok"][l][:, :, a:b], b - a
                            else:
                                a = (c - len(TOKC)) * 384
                                src, w = A["w_gdn"][l][:, :, a:a + 384], 384
                            sp.dma_start(wt[:, r, :, 0:w], src).then_inc(w_in[r], 16)

                        for i in range(NT):
                            if i >= 2:
                                sp.wait_ge(h_ready, i - 1)
                                sp.wait_ge(sq_done, i - 1)
                            sp.dma_start(xt[:, i % 2], xres[i * P:(i + 1) * P, :]).then_inc(x_in[i % 2], 16)
                            if i < RING:
                                load_w(i)
                        for c in range(RING, NCH):
                            load_w(c)

                    @block.gpsimd
                    def _(pool):
                        nc.gpsimd.memset(mh[:, :], -0.5).then_inc(ch_zero, 1)
                        for a, b in ((0, PAD), (PAD + SEQ, CTX0), (CW - PAD, CW)):
                            nc.gpsimd.memset(chan[:, :, a:b], 0.0).then_inc(ch_zero, 1)
                        pool.wait_ge(ch_zero, 4)
                        for i in range(NT):
                            pool.wait_ge(ms_done, i + 1)
                            nc.gpsimd.tensor_tensor(rs[:, i:i + 1], ss[:, i:i + 1], mh[:, :], ALU.pow).then_inc(rstd, 1)

                    @block.scalar
                    def _(act):
                        def square(i):
                            act.wait_ge(x_in[i % 2], 16 * (i // 2) + 16)
                            if i:
                                act.wait_ge(sq_done, i)
                            nc.scalar.activation(sq[:, :], xt[:, i % 2], ACT.Square, accum_out=ss[:, i:i + 1]).then_inc(sq_done, 1)

                        square(0)
                        for i in range(NT):
                            if i + 1 < NT:
                                square(i + 1)
                            act.wait_ge(turned, i + 1)
                            b = 2 * (i % 2)
                            nc.scalar.copy(hT[:, :, i * P:(i + 1) * P],
                                           psum[:, b:b + 2, :].rearrange("p b (k t) -> p (b k) t", t=P)).then_inc(hT_ready, 1)
                        for n, it in enumerate(items):
                            if n % 2:
                                act.wait_ge(prod, n + 1)
                                nc.scalar.copy(dest(it), psum[:, 4 + n % 4, 0:width(it)]).then_inc(out_s, 1)

                    @block.vector
                    def _(dve):
                        ch = Chain(dve, step)
                        for i in range(NT):
                            s = 0 if i < NLT else 1
                            dve.wait_ge(sq_done, i + 1)
                            nc.vector.tensor_scalar(ss[:, i:i + 1], ss[:, i:i + 1], 1.0 / D, EPS, ALU.mult, ALU.add).then_inc(ms_done, 1)
                            dve.wait_ge(rstd, i + 1)
                            if i >= 2:
                                dve.wait_ge(turned, i - 1)
                            ch(nc.vector.scalar_tensor_tensor(out=hh[:, i % 2], in0=xt[:, i % 2], scalar=rs[:, i:i + 1],
                                                              in1=rows[:, 0, s], op0=ALU.mult, op1=ALU.mult))
                            nc.vector.tensor_tensor(hh[:, i % 2], hh[:, i % 2], rows[:, 1, s], ALU.add).then_inc(h_ready, 1)
                        for n, it in enumerate(items):
                            if n % 2 == 0:
                                dve.wait_ge(prod, n + 1)
                                nc.vector.tensor_copy(dest(it), psum[:, 4 + n % 4, 0:width(it)]).then_inc(out_v, 1)

                    @block.tensor
                    def _(pe):
                        for i in range(NT):
                            pe.wait_ge(h_ready, i + 1)
                            if i >= 2:
                                pe.wait_ge(hT_ready, i - 1)
                            for k in range(DK):
                                last = nc.tensor.transpose(psum[:, 2 * (i % 2) + k // 4, (k % 4) * P:(k % 4 + 1) * P],
                                                           hh[:, i % 2, k * P:(k + 1) * P], cst("ident"))
                            last.then_inc(turned, 1)
                        pe.wait_ge(hT_ready, NT)
                        for n, it in enumerate(items):
                            c, kind, i, a, b = it
                            pe.wait_ge(w_in[c % RING], 16 * (c // RING) + 16)
                            if n >= 4:
                                pe.wait_ge(out_s if n % 2 else out_v, (n - 4) // 2 + 1)
                            for k in range(DK):
                                if kind == "tok":
                                    lhsT, rhs = hT[:, k, i * P:(i + 1) * P], wt[:, c % RING, k, 0:b - a]
                                else:
                                    lhsT = wt[:, c % RING, k, b * P:(b + 1) * P]
                                    rhs = hT[:, k, 0:SEQ] if a == 0 else hT[:, k, SEQ:NTOK]
                                last = nc.tensor.matmul(psum[:, 4 + n % 4, 0:width(it)], lhsT, rhs,
                                                        start=(k == 0), stop=(k == DK - 1))
                            last.then_inc(prod, 1)
                S.end()

        def phase_gdn_features(l, chan, feat, gqT, gkT):
            CO = CW - 2 * PAD
            st, S = ExitStack(), Sems(nc, f"gf{l}")
            with st:
                acc = sbuf(st, "acc", [P, 2, CO])
                cs = sbuf(st, "cs", [P, 2, CO])
                sq = sbuf(st, "sqf", [P, 2, 12 * HD])
                nrm = sbuf(st, "nrm", [P, NT, 12])
                mh = sbuf(st, "mh2", [P, 12])
                step, conv_done, silu_done, turned, feat_ready = S("step"), S("conv_done"), S("silu_done"), S("turned"), S("feat_ready")
                sq_done, ss_done, rn_done, unit_done = S("sq_done"), S("ss_done"), S("rn_done"), S("unit_done")
                turned2, out2, mh_set = S("turned2"), S("out2"), S("mh_set")
                NQK = 2 * GH * HD
                with nc.Block() as block:
                    @block.vector
                    def _(dve):
                        ch = Chain(dve, step)
                        for j in range(NGT):
                            if j >= 2:
                                dve.wait_ge(silu_done, j - 1)
                            a = acc[:, j % 2]
                            w = lambda t: par(l, "conv", j * CONV + t, j * CONV + t + 1)
                            ch(nc.vector.tensor_scalar(a, chan[:, j, 0:CO], w(0), None, ALU.mult))
                            for t in range(1, CONV):
                                ins = nc.vector.scalar_tensor_tensor(out=a, in0=chan[:, j, t:t + CO], scalar=w(t), in1=a,
                                                                     op0=ALU.mult, op1=ALU.add)
                                if t < CONV - 1:
                                    ch(ins)
                                else:
                                    ins.then_inc(conv_done, 1)
                        for i in range(NT):
                            dve.wait_ge(sq_done, i + 1)
                            ch(nc.vector.tensor_reduce(nrm[:, i], sq[:, i % 2].rearrange("p (h d) -> p h d", d=HD), AX.X, ALU.add))
                            nc.vector.tensor_scalar(nrm[:, i], nrm[:, i], EPS, None, ALU.add).then_inc(ss_done, 1)
                        for i in range(NT):
                            dve.wait_ge(rn_done, i + 1)
                            ch(nc.vector.tensor_scalar(nrm[:, i, 0:GH], nrm[:, i, 0:GH], HD ** -0.5, None, ALU.mult))
                            v = feat[:, i, 0:NQK].rearrange("p (h d) -> p h d", d=HD)
                            nc.vector.tensor_tensor(v, v, nrm[:, i].unsqueeze(2).to_broadcast([P, 12, HD]), ALU.mult).then_inc(unit_done, 1)

                    @block.gpsimd
                    def _(pool):
                        nc.gpsimd.memset(mh[:, :], -0.5).then_inc(mh_set, 1)
                        pool.wait_ge(mh_set, 1)
                        for i in range(NT):
                            pool.wait_ge(ss_done, i + 1)
                            nc.gpsimd.tensor_tensor(nrm[:, i], nrm[:, i], mh[:, :], ALU.pow).then_inc(rn_done, 1)

                    @block.scalar
                    def _(act):
                        def silu(j):
                            act.wait_ge(conv_done, j + 1)
                            if j >= 2:
                                act.wait_ge(turned, j - 1)
                            nc.scalar.activation(cs[:, j % 2], acc[:, j % 2], ACT.Silu).then_inc(silu_done, 1)

                        silu(0)
                        for j in range(NGT):
                            if j + 1 < NGT:
                                silu(j + 1)
                            act.wait_ge(turned, j + 1)
                            b = 2 * (j % 2)
                            flat = psum[:, b:b + 2, :].rearrange("p b n -> p (b n)")[:, 0:NTOK]
                            nc.scalar.copy(feat[:, :, j * P:(j + 1) * P], flat.rearrange("p (i n) -> p i n", n=P)).then_inc(feat_ready, 1)
                        act.wait_ge(feat_ready, NGT)
                        for i in range(NT):
                            if i >= 2:
                                act.wait_ge(ss_done, i - 1)
                            nc.scalar.activation(sq[:, i % 2], feat[:, i, 0:NQK], ACT.Square).then_inc(sq_done, 1)
                        for i in range(NT):
                            act.wait_ge(turned2, i + 1)
                            b = 4 + 2 * (i % 2)
                            flat = psum[:, b:b + 2, :].rearrange("p b n -> p (b n)")
                            nc.scalar.copy(gqT[:, :, i * P:(i + 1) * P], flat[:, 0:384].rearrange("p (m n) -> p m n", n=P))
                            nc.scalar.copy(gkT[:, :, i * P:(i + 1) * P], flat[:, 384:768].rearrange("p (m n) -> p m n", n=P)).then_inc(out2, 1)

                    @block.tensor
                    def _(pe):
                        for j in range(NGT):
                            pe.wait_ge(silu_done, j + 1)
                            if j >= 2:
                                pe.wait_ge(feat_ready, j - 1)
                            for i in range(NT):
                                c = tile_col(i) - PAD
                                last = nc.tensor.transpose(psum[:, 2 * (j % 2) + i // 4, (i % 4) * P:(i % 4 + 1) * P],
                                                           cs[:, j % 2, c:c + P], cst("ident"))
                            last.then_inc(turned, 1)
                        for i in range(NT):
                            pe.wait_ge(unit_done, i + 1)
                            if i >= 2:
                                pe.wait_ge(out2, i - 1)
                            for m in range(6):
                                last = nc.tensor.transpose(psum[:, 4 + 2 * (i % 2) + m // 4, (m % 4) * P:(m % 4 + 1) * P],
                                                           feat[:, i, m * P:(m + 1) * P], cst("ident"))
                            last.then_inc(turned2, 1)
                S.end()

        def phase_attention_features(l, patt, sqT, skT, mqT, mkT, mv):
            st, S = ExitStack(), Sems(nc, f"af{l}")
            NR = SWA_H + SWA_KV
            with st:
                wuq = sbuf(st, "wuq", [P, 2, MH * MQ])
                wukv = sbuf(st, "wukv", [P, MH * (MNOPE + HD)])
                t = sbuf(st, "rt", [P, NR * HD])
                u = sbuf(st, "ru", [P, NR * HD])
                rqk = sbuf(st, "rqk", [P, 2, NR * HD])
                junk = sbuf(st, "junk", [P, QR])
                ss = sbuf(st, "ssm", [P, NT, 2])
                mh = sbuf(st, "mh3", [P, 2])
                cn = sbuf(st, "cn", [P, 2, QR + KVR])
                cT = sbuf(st, "cT", [P, 2, 3 * P])
                kr = sbuf(st, "kr", [P, MROPE])
                qm = sbuf(st, "qm", [P, 2, MH, MQ])
                km = sbuf(st, "km", [P, 2, MH, MQ])
                w_in, step, mh_set, sq_done, ms_done, rs_done = S("w_in"), S("step"), S("mh_set"), S("sq_done"), S("ms_done"), S("rs_done")
                rope_done, cn_done, turned1, copied1 = S("rope_done"), S("cn_done"), S("turned1"), S("copied1")
                up_done, kv_copied, qk_done, turned2, copied2 = S("up_done"), S("kv_copied"), S("qk_done"), S("turned2"), S("copied2")
                with nc.Block() as block:
                    @block.sync
                    def _(sp):
                        sp.dma_start(wuq[:, 0, :], A["w_uq"][l, 0:P, :]).then_inc(w_in, 16)
                        sp.dma_start(wuq[0:QR - P, 1, :], A["w_uq"][l, P:QR, :]).then_inc(w_in, 16)
                        sp.dma_start(wukv[:, :], A["w_ukv"][l]).then_inc(w_in, 16)

                    @block.gpsimd
                    def _(pool):
                        nc.gpsimd.memset(mh[:, :], -0.5).then_inc(mh_set, 1)
                        pool.wait_ge(mh_set, 1)
                        for i in range(NT):
                            pool.wait_ge(ms_done, i + 1)
                            nc.gpsimd.tensor_tensor(ss[:, i], ss[:, i], mh[:, :], ALU.pow).then_inc(rs_done, 1)

                    @block.vector
                    def _(dve):
                        ch = Chain(dve, step)

                        def rotate(x, n, table, dim, i, tt, uu):
                            q = dim // 4
                            cos = cst(table, i * dim, (i + 1) * dim)
                            sin = cst(table, (NT + i) * dim, (NT + i + 1) * dim).rearrange("p (f s n) -> p f s n", f=2, s=2)
                            ch(nc.vector.tensor_tensor(tt, x, cos.unsqueeze(1).to_broadcast([P, n, dim]), ALU.mult))
                            xv = x.rearrange("p h (f s n) -> p h f s n", f=2, s=2)
                            uv = uu.rearrange("p h (f s n) -> p h f s n", f=2, s=2)
                            for s in range(2):
                                ch(nc.vector.tensor_tensor(uv[:, :, :, s], xv[:, :, :, 1 - s],
                                                           sin[:, :, s].unsqueeze(1).to_broadcast([P, n, 2, q]), ALU.mult))

                        for i in range(NT):
                            dve.wait_ge(sq_done, i + 1)
                            ch(nc.vector.tensor_scalar(ss[:, i, 0:1], ss[:, i, 0:1], 1.0 / QR, EPS, ALU.mult, ALU.add))
                            nc.vector.tensor_scalar(ss[:, i, 1:2], ss[:, i, 1:2], 1.0 / KVR, EPS, ALU.mult, ALU.add).then_inc(ms_done, 1)
                        for i in range(NT):
                            hv = lambda a: a.rearrange("p (h d) -> p h d", d=HD)
                            rotate(hv(patt[:, i, 0:NR * HD]), NR, "rope_swa", HD, i, hv(t[:, :]), hv(u[:, :]))
                            if i >= 2:
                                dve.wait_ge(turned1, i - 1)
                            pair = lambda a: a[:, 0:O_K].rearrange("p (g j d) -> p g j d", g=2, d=HD)
                            dst = rqk[:, i % 2, 0:O_K].rearrange("p (j g d) -> p g j d", g=2, d=HD)
                            for g in range(2):
                                ch(nc.vector.tensor_tensor(dst[:, g], pair(t)[:, g], pair(u)[:, g], ALU.add))
                            ch(nc.vector.tensor_tensor(rqk[:, i % 2, O_K:O_V], t[:, O_K:O_V], u[:, O_K:O_V], ALU.add))
                            dve.wait_ge(rs_done, i + 1)
                            ch(nc.vector.scalar_tensor_tensor(out=cn[:, i % 2, 0:QR], in0=patt[:, i, O_CQ:O_CKV], scalar=ss[:, i, 0:1],
                                                              in1=par(l, "q_norm"), op0=ALU.mult, op1=ALU.mult))
                            nc.vector.scalar_tensor_tensor(out=cn[:, i % 2, QR:QR + KVR], in0=patt[:, i, O_CKV:O_KR], scalar=ss[:, i, 1:2],
                                                           in1=par(l, "kv_norm"), op0=ALU.mult, op1=ALU.mult).then_inc(cn_done, 1)
                            rotate(patt[:, i, O_KR:W_ATT].unsqueeze(1), 1, "rope_mla", MROPE, i,
                                   t[:, 0:MROPE].unsqueeze(1), u[:, 0:MROPE].unsqueeze(1))
                            ch(nc.vector.tensor_tensor(kr[:, :], t[:, 0:MROPE], u[:, 0:MROPE], ALU.add))
                            if i >= 2:
                                dve.wait_ge(turned2, i - 1)
                            dve.wait_ge(up_done, i + 1)
                            qp = psum[:, 2, 0:MH * MQ].rearrange("p (h d) -> p h d", d=MQ)
                            kp = psum[:, 3, :].rearrange("p (h d) -> p h d", h=MH)
                            tv = t[:, 0:MH * MROPE].rearrange("p (h d) -> p h d", h=MH)
                            uv = u[:, 0:MH * MROPE].rearrange("p (h d) -> p h d", h=MH)
                            rotate(qp[:, :, MNOPE:MQ], MH, "rope_mla", MROPE, i, tv, uv)
                            ch(nc.vector.tensor_tensor(qm[:, i % 2, :, MNOPE:MQ], tv, uv, ALU.add))
                            ch(nc.vector.tensor_copy(qm[:, i % 2, :, 0:MNOPE], qp[:, :, 0:MNOPE]))
                            ch(nc.vector.tensor_copy(km[:, i % 2, :, 0:MNOPE], kp[:, :, 0:MNOPE]))
                            ch(nc.vector.tensor_copy(mv[:, i], kp[:, :, MNOPE:]))
                            nc.vector.tensor_copy(km[:, i % 2, :, MNOPE:MQ], kr[:, :].unsqueeze(1).to_broadcast([P, MH, MROPE])).then_inc(qk_done, 1)
                            dve.wait_ge(qk_done, i + 1)

                    @block.scalar
                    def _(act):
                        for i in range(NT):
                            if i:
                                act.wait_ge(sq_done, i)
                            nc.scalar.activation(junk[:, :], patt[:, i, O_CQ:O_CKV], ACT.Square, accum_out=ss[:, i, 0:1]).then_inc(kv_copied, 1)
                            act.wait_ge(kv_copied, i + 1)
                            nc.scalar.activation(junk[:, 0:KVR], patt[:, i, O_CKV:O_KR], ACT.Square, accum_out=ss[:, i, 1:2]).then_inc(sq_done, 1)
                        for i in range(NT):
                            act.wait_ge(turned1, i + 1)
                            sl = slice(i * P, (i + 1) * P)
                            nc.scalar.copy(cT[:, i % 2, 0:P], psum[:, 1, 0:P])
                            nc.scalar.copy(cT[0:QR - P, i % 2, P:2 * P], psum[0:QR - P, 1, P:2 * P])
                            nc.scalar.copy(cT[:, i % 2, 2 * P:3 * P], psum[:, 1, 2 * P:3 * P])
                            nc.scalar.copy(sqT[:, :, sl], psum[:, 0, 0:3 * P].rearrange("p (m n) -> p m n", n=P))
                            nc.scalar.copy(skT[:, sl], psum[:, 0, 3 * P:4 * P]).then_inc(copied1, 1)
                            act.wait_ge(turned2, i + 1)
                            nc.scalar.copy(mqT[0:MQ, :, sl], psum[0:MQ, 4, :].rearrange("p (m n) -> p m n", n=P))
                            nc.scalar.copy(mkT[0:MQ, :, sl], psum[0:MQ, 5, :].rearrange("p (m n) -> p m n", n=P)).then_inc(copied2, 1)

                    @block.tensor
                    def _(pe):
                        pe.wait_ge(w_in, 48)
                        for i in range(NT):
                            pe.wait_ge(cn_done, i + 1)
                            if i:
                                pe.wait_ge(copied1, i)
                            for m in range(4):
                                nc.tensor.transpose(psum[:, 0, m * P:(m + 1) * P], rqk[:, i % 2, m * P:(m + 1) * P], cst("ident"))
                            nc.tensor.transpose(psum[:, 1, 0:P], cn[:, i % 2, 0:P], cst("ident"))
                            nc.tensor.transpose(psum[0:QR - P, 1, P:2 * P], cn[:, i % 2, P:QR], cst("ident"))
                            nc.tensor.transpose(psum[:, 1, 2 * P:3 * P], cn[:, i % 2, QR:QR + KVR], cst("ident")).then_inc(turned1, 1)
                            pe.wait_ge(copied1, i + 1)
                            if i:
                                pe.wait_ge(qk_done, i)
                            nc.tensor.matmul(psum[:, 2, 0:MH * MQ], cT[:, i % 2, 0:P], wuq[:, 0, :], start=True, stop=False)
                            nc.tensor.matmul(psum[:, 2, 0:MH * MQ], cT[0:QR - P, i % 2, P:2 * P], wuq[0:QR - P, 1, :], start=False, stop=True)
                            nc.tensor.matmul(psum[:, 3, :], cT[:, i % 2, 2 * P:3 * P], wukv[:, :], start=True, stop=True).then_inc(up_done, 1)
                            pe.wait_ge(qk_done, i + 1)
                            if i:
                                pe.wait_ge(copied2, i)
                            for h in range(MH):
                                nc.tensor.transpose(psum[0:MQ, 4, h * P:(h + 1) * P], qm[:, i % 2, h, :], cst("ident"))
                                last = nc.tensor.transpose(psum[0:MQ, 5, h * P:(h + 1) * P], km[:, i % 2, h, :], cst("ident"))
                            last.then_inc(turned2, 1)
                S.end()

        def phase_attention(l, nq, patt, sqT, skT, mqT, mkT, mv, cat):
            units = []
            for h in range(SWA_H + MH):
                for i in range(nq):
                    swa = h < SWA_H
                    if i >= NLT:
                        local = []
                    elif swa:
                        local = list(range(max(i - 1, 0), min(i + 2, NLT)))
                    else:
                        local = list(range(NLT))
                    units.append((h, i, swa, local, local + list(range(NLT, NT))))
            NU = len(units)
            st, S = ExitStack(), Sems(nc, f"at{l}")
            with st:
                E = sbuf(st, "E", [P, 2, NTOK])
                ET = sbuf(st, "ET", [P, 2, NTOK])
                mx = sbuf(st, "mx", [P, 4])
                nb = sbuf(st, "nb", [P, 2])
                es = sbuf(st, "es", [P, 4, 2])
                den = sbuf(st, "den", [P, 4])
                cat_out = S("cat_out")
                step, scored, nb_done, exp_done, turned, et_done, pv_done, out_done = (
                    S("step"), S("scored"), S("nb_done"), S("exp_done"), S("turned"), S("et_done"), S("pv_done"), S("out_done"))
                sflat = lambda u: psum[:, 2 * (u % 2):2 * (u % 2) + 2, :].rearrange("p b n -> p (b n)")
                span = lambda un: (512 - P * len(un[3]), 512 + CTXN)
                tflat = psum[:, 4:6, :].rearrange("p b n -> p (b n)")
                with nc.Block() as block:
                    @block.sync
                    def _(sp):
                        sp.wait_ge(out_done, NU)
                        for a, b in ((0, SWA_H * HD), ((SWA_H + GH) * HD, D)):
                            sp.dma_start(cat_dram[0:nq * P, a:b].rearrange("(i p) n -> p i n", p=P), cat[:, :, a:b]).then_inc(cat_out, 16)
                        sp.wait_ge(cat_out, 32)

                    @block.tensor
                    def _(pe):
                        def score(u):
                            h, i, swa, local, keys = units[u]
                            if u >= 2:
                                pe.wait_ge(exp_done, u - 1)
                            if swa:
                                g, j = h // 3, h % 3
                                q, k = sqT[64 * g:64 * g + 64, j, i * P:(i + 1) * P], skT[64 * g:64 * g + 64, :]
                            else:
                                q, k = mqT[0:MQ, h - SWA_H, i * P:(i + 1) * P], mkT[0:MQ, h - SWA_H, :]
                            s = sflat(u)
                            if local:
                                nc.tensor.matmul(s[:, span(units[u])[0]:512], q, k[:, local[0] * P:(local[-1] + 1) * P], start=True, stop=True)
                            nc.tensor.matmul(s[:, 512:512 + CTXN], q, k[:, SEQ:NTOK], start=True, stop=True).then_inc(scored, 1)

                        def turn(u):
                            pe.wait_ge(exp_done, u + 1)
                            n = len(units[u][4])
                            for c in range(n):
                                last = nc.tensor.transpose(tflat[:, c * P:(c + 1) * P], E[:, u % 2, c * P:(c + 1) * P], cst("ident"))
                            last.then_inc(turned, 1)

                        def values(u):
                            h, i, swa, local, keys = units[u]
                            pe.wait_ge(et_done, u + 1)
                            if u >= 2:
                                pe.wait_ge(out_done, u - 1)
                            for c, kt in enumerate(keys):
                                v = patt[:, kt, O_V + (h // 3) * HD:O_V + (h // 3 + 1) * HD] if swa else mv[:, kt, h - SWA_H, :]
                                last = nc.tensor.matmul(psum[:, 6 + u % 2, 0:HD], ET[:, u % 2, c * P:(c + 1) * P], v,
                                                        start=(c == 0), stop=(c == len(keys) - 1))
                            last.then_inc(pv_done, 1)

                        score(0)
                        for u in range(NU):
                            if u + 1 < NU:
                                score(u + 1)
                            if u:
                                values(u - 1)
                            turn(u)
                        values(NU - 1)

                    @block.vector
                    def _(dve):
                        ch = Chain(dve, step)

                        def bias(u):
                            h, i, swa, local, keys = units[u]
                            a, b = span(units[u])
                            s = sflat(u)
                            dve.wait_ge(scored, u + 1)
                            if swa and i < NLT:
                                for kt, name in ((i - 1, "prev"), (i + 1, "next")):
                                    if kt in local:
                                        c = a + (kt - local[0]) * P
                                        ch(nc.vector.tensor_tensor(s[:, c:c + P], s[:, c:c + P], cst(name), ALU.add))
                            ch(nc.vector.reduce_max(mx[:, u % 2:u % 2 + 1], s[:, a:b], AX.X))
                            if u >= 2:
                                dve.wait_ge(exp_done, u - 1)
                            m, o = mx[:, u % 2:u % 2 + 1], nb[:, u % 2:u % 2 + 1]
                            if swa:
                                ch(nc.vector.tensor_scalar(m, m, HD ** -0.5, par(l, "sink", h, h + 1), ALU.mult, ALU.max))
                                nc.vector.tensor_scalar(o, m, -1.0, None, ALU.mult).then_inc(nb_done, 1)
                            else:
                                nc.vector.tensor_scalar(o, m, -(MQ ** -0.5), None, ALU.mult).then_inc(nb_done, 1)

                        def norm(u):
                            dve.wait_ge(exp_done, u + 1)
                            d = den[:, u % 4:u % 4 + 1]
                            if units[u][2]:
                                ch(nc.vector.tensor_tensor(es[:, u % 4, 0:1], es[:, u % 4, 0:1], es[:, u % 4, 1:2], ALU.add))
                            ch(nc.vector.reciprocal(d, es[:, u % 4, 0:1]))

                        def write(u):
                            h, i = units[u][0:2]
                            c = h * HD if h < SWA_H else (SWA_H + GH + h - SWA_H) * HD
                            dve.wait_ge(pv_done, u + 1)
                            nc.vector.tensor_scalar(cat[:, i, c:c + HD], psum[:, 6 + u % 2, 0:HD], den[:, u % 4:u % 4 + 1], None,
                                                    ALU.mult).then_inc(out_done, 1)
                            dve.wait_ge(out_done, u + 1)

                        for u in range(NU):
                            bias(u)
                            if u >= 2:
                                write(u - 2)
                            if u >= 1:
                                norm(u - 1)
                        if NU >= 2:
                            write(NU - 2)
                        norm(NU - 1)
                        write(NU - 1)

                    @block.scalar
                    def _(act):
                        def exps(u):
                            h, i, swa, local, keys = units[u]
                            a, b = span(units[u])
                            act.wait_ge(nb_done, u + 1)
                            if u >= 2:
                                act.wait_ge(turned, u - 1)
                            bias = nb[:, u % 2:u % 2 + 1]
                            if swa:
                                nc.scalar.activation(es[:, u % 4, 1:2], par(l, "sink", h, h + 1), ACT.Exp, bias=bias)
                            nc.scalar.activation(E[:, u % 2, 0:b - a], sflat(u)[:, a:b], ACT.Exp, bias=bias,
                                                 scale=HD ** -0.5 if swa else MQ ** -0.5,
                                                 accum_out=es[:, u % 4, 0:1]).then_inc(exp_done, 1)

                        for u in range(min(2, NU)):
                            exps(u)
                        for u in range(NU):
                            n = len(units[u][4]) * P
                            act.wait_ge(turned, u + 1)
                            if u >= 2:
                                act.wait_ge(pv_done, u - 1)
                            nc.scalar.copy(ET[:, u % 2, 0:n], tflat[:, 0:n]).then_inc(et_done, 1)
                            if u + 2 < NU:
                                exps(u + 2)
                S.end()

        def phase_gdn_prepare(l, zb, feat, gqT, gkT, U, WT, QT, IT, KO, gS):
            st, S = ExitStack(), Sems(nc, f"gp{l}")
            FULL = NT + NT * TOPK
            H2 = 2 * GH
            B0 = GH * HD
            with st:
                kg = sbuf(st, "kg", [P, 2, GH * HD])
                qe = sbuf(st, "qe", [P, 2, GH * HD])
                trig = sbuf(st, "trig", [P, 2, 3 * P])
                E = sbuf(st, "Ed", [P, 2, 3 * P])
                LT = [sbuf(st, f"LT{r}", [P, 2, 3 * P]) for r in range(2)]
                X = sbuf(st, "Xl", [P, 2, 3 * P])
                DD = sbuf(st, "DD", [P, 2, 3 * P])
                DT = sbuf(st, "DT", [P, 2, 3 * P])
                g = sbuf(st, "g", [P, NT, H2])
                beta = sbuf(st, "beta", [P, NT, H2])
                na = sbuf(st, "na", [P, H2])
                gc = sbuf(st, "gc", [P, NT, H2])
                eg = sbuf(st, "eg", [P, NT, H2])
                ek = sbuf(st, "ek", [P, NT, H2])
                tmp = ek
                step, astep, g_ready, sums, gc_ready = S("step"), S("astep"), S("g_ready"), S("sums"), S("gc_ready")
                eg_ready, ko_done, kg_done, qe_done, q_turned, q_copied, s_ready = (
                    S("eg_ready"), S("ko_done"), S("kg_done"), S("qe_done"), S("q_turned"), S("q_copied"), S("s_ready"))
                trig_done, rowed, dif_done, exp_done, kk_done, lt_done = (
                    S("trig_done"), S("rowed"), S("dif_done"), S("exp_done"), S("kk_done"), S("lt_done"))
                x_prod, x_done, d_prod, dt_prod, dt_done = S("x_prod"), S("x_done"), S("d_prod"), S("dt_prod"), S("dt_done")
                end_prod, end_copied, ek_ready, d_done = S("end_prod"), S("end_copied"), S("ek_ready"), S("d_done")
                units = [(i, par_) for i in range(NT) for par_ in range(2)]
                b3 = lambda ap: ap.unsqueeze(1).to_broadcast([P, 3, P])
                v3 = lambda ap: ap.rearrange("p (m n) -> p m n", n=P)
                flat = lambda ap: ap.rearrange("p i h -> p (i h)")
                filled = S("filled")
                with nc.Block() as block:
                    @block.sync
                    def _(sp):
                        if l == 0:
                            for b in range(FULL, NBMAX, 8):
                                sp.dma_start(y_dram[b * P:(b + 8) * P, :].rearrange("(b p) d -> p b d", p=P),
                                             const[:, 0:D].unsqueeze(1).to_broadcast([P, 8, D])).then_inc(filled, 16)
                            sp.wait_ge(filled, 16 * (NBMAX - FULL) // 8)

                    @block.scalar
                    def _(act):
                        ch = Chain(act, astep)
                        a = zb[:, :, B0 + H2:B0 + 2 * H2]
                        ch(nc.scalar.activation(beta[:, :, :], zb[:, :, B0:B0 + H2], ACT.Sigmoid))
                        ch(nc.scalar.activation(na[:, :], par(l, "a_log"), ACT.Exp))
                        act.wait_ge(step, 1)
                        ch(nc.scalar.activation(tmp[:, :, :], g[:, :, :], ACT.Abs))
                        ch(nc.scalar.activation(tmp[:, :, :], tmp[:, :, :], ACT.Exp, scale=-1.0))
                        ch(nc.scalar.activation(tmp[:, :, :], tmp[:, :, :], ACT.Ln, bias=1.0))
                        act.wait_ge(gc_ready, 1)
                        ch(nc.scalar.activation(eg[:, :, :], gc[:, :, :], ACT.Exp))
                        ch(nc.scalar.activation(ek[:, :, :], ek[:, :, :], ACT.Exp))
                        for r in range(2):
                            for q in range(2):
                                src = psum[64 * q:64 * q + 64, 2 + r, 0:NT * H2].rearrange("p (i d m q) -> p i d m q", d=2, m=3, q=2)
                                ins = nc.scalar.activation(gS[64 * q:64 * q + 64, :, r], src[:, :, :, :, q], ACT.Exp)
                                if (r, q) == (1, 1):
                                    ins.then_inc(eg_ready, 1)
                                else:
                                    ch(ins)

                        def tail(n):
                            i, par_ = units[n // 2]
                            d = n % 2
                            act.wait_ge(end_prod, n + 1)
                            uv = U[:, i, d].rearrange("p (m q e) -> p m q e", q=2, e=HD)[:, :, par_]
                            nc.scalar.copy(uv, psum[:, 2 + d, 0:3 * HD].rearrange("p (m e) -> p m e", e=HD))
                            ph = slice(64 * par_, 64 * par_ + 64)
                            nc.scalar.copy(WT[ph, i, d], psum[ph, 4 + d, 0:3 * P]).then_inc(end_copied, 1)

                        def decay(u):
                            for d in range(2):
                                act.wait_ge(dif_done, 2 * u + d + 1)
                                nc.scalar.activation(E[:, d], E[:, d], ACT.Exp).then_inc(exp_done, 1)

                        decay(0)
                        for u in range(len(units)):
                            if u < NT:
                                for d in range(2):
                                    act.wait_ge(q_turned, 2 * u + d + 1)
                                    nc.scalar.copy(QT[:, u, d], psum[:, 6 + d, 0:3 * P]).then_inc(q_copied, 1)
                            if u + 1 < len(units):
                                decay(u + 1)
                            tail(2 * u)
                            tail(2 * u + 1)

                    @block.gpsimd
                    def _(pool):
                        def scaled(out_, src, sc, i, d):
                            return nc.gpsimd.tensor_tensor(out_.rearrange("p (h e) -> p h e", e=HD), src.rearrange("p (h e) -> p h e", e=HD),
                                                           sc[:, i, d * GH:(d + 1) * GH].unsqueeze(2).to_broadcast([P, GH, HD]), ALU.mult)

                        pool.wait_ge(eg_ready, 1)
                        pool.wait_ge(ek_ready, 1)
                        for n in range(2 * len(units)):
                            i, par_ = units[n // 2]
                            d = n % 2
                            if n >= 2:
                                pool.wait_ge(rowed, n - 1)
                            gh = g[:, i, d * GH:(d + 1) * GH].rearrange("p (m q) -> p m q", q=2)[:, :, par_]
                            nc.gpsimd.tensor_tensor(v3(trig[:, d]), b3(cst("tri", d * P, (d + 1) * P)),
                                                    gh.unsqueeze(2).to_broadcast([P, 3, P]), ALU.mult).then_inc(trig_done, 1)
                            if n // 2 < NT:
                                ii = n // 2
                                m = 2 * ii + d
                                if m >= 2:
                                    pool.wait_ge(q_turned, m - 1)
                                scaled(qe[:, d], feat[:, ii, 0:GH * HD], eg, ii, d).then_inc(qe_done, 1)
                            if par_ == 1:
                                if i:
                                    pool.wait_ge(end_prod, 4 * i)
                                scaled(kg[:, d], feat[:, i, GH * HD:2 * GH * HD], eg, i, d).then_inc(kg_done, 1)
                                scaled(KO[:, i, d], feat[:, i, GH * HD:2 * GH * HD], ek, i, d).then_inc(ko_done, 1)

                    @block.tensor
                    def _(pe):
                        pe.wait_ge(g_ready, 1)
                        gv = flat(g[:, :, :])
                        for d in range(2):
                            nc.tensor.matmul(psum[:, d, 0:NT * GH], cst("tri", d * P, (d + 1) * P),
                                             g[:, :, d * GH:(d + 1) * GH], start=True, stop=True)
                        nc.tensor.matmul(psum[:, 4, 0:NT * H2], cst("chunk"), gv, start=True, stop=True)
                        for r in range(2):
                            last = nc.tensor.matmul(psum[:, 2 + r, 0:NT * H2], cst("half", r * P, (r + 1) * P), gv, start=True, stop=True)
                        last.then_inc(sums, 1)
                        pe.wait_ge(gc_ready, 1)
                        pe.wait_ge(eg_ready, 1)

                        def gate_rows(u):
                            for d in range(2):
                                n = 2 * u + d
                                pe.wait_ge(trig_done, n + 1)
                                if u:
                                    pe.wait_ge(lt_done, 2 * u)
                                nc.tensor.matmul(psum[:, d, 0:3 * P], cst("ones"), trig[:, d], start=True, stop=True).then_inc(rowed, 1)

                        def products(u):
                            i, par_ = units[u]
                            sl = slice(i * P, (i + 1) * P)
                            ph = slice(64 * par_, 64 * par_ + 64)
                            pe.wait_ge(dif_done, 2 * u + 2)
                            for m in range(3):
                                nc.tensor.matmul(psum[:, 0, m * P:(m + 1) * P], gkT[ph, m, sl], gkT[ph, m, sl], start=True, stop=True)
                            for m in range(3):
                                last = nc.tensor.matmul(psum[:, 1, m * P:(m + 1) * P], gkT[ph, m, sl], gqT[ph, m, sl], start=True, stop=True)
                            last.then_inc(kk_done, 1)

                        def turn_q(i):
                            for d in range(2):
                                m = 2 * i + d
                                pe.wait_ge(qe_done, m + 1)
                                for c in range(3):
                                    last = nc.tensor.transpose(psum[:, 6 + d, c * P:(c + 1) * P], qe[:, d, c * P:(c + 1) * P], cst("ident"))
                                last.then_inc(q_turned, 1)

                        gate_rows(0)
                        products(0)
                        for u in range(len(units)):
                            i, par_ = units[u]
                            if u < NT:
                                if u:
                                    pe.wait_ge(dt_done, NLEV * 2 * u)
                                turn_q(u)
                                pe.wait_ge(q_copied, 2 * u + 2)
                            for v in range(NLEV):
                                for d in range(2):
                                    n = (NLEV * u + v) * 2 + d
                                    if v == 0:
                                        pe.wait_ge(lt_done, 2 * u + d + 1)
                                        if u:
                                            pe.wait_ge(end_copied, 2 * (u - 1) + d + 1)
                                    else:
                                        pe.wait_ge(d_done, (NLEV - 1) * 2 * u + 2 * (v - 1) + d + 1)
                                    for m in range(3):
                                        c = slice(m * P, (m + 1) * P)
                                        last = nc.tensor.matmul(psum[:, 2 + d, c], LT[u % 2][:, d, c], DD[:, d, c] if v else cst("ident"), start=True, stop=True)
                                    last.then_inc(x_prod, 1)
                                for d in range(2):
                                    n = (NLEV * u + v) * 2 + d
                                    if v == 0:
                                        continue
                                    pe.wait_ge(x_done, n + 1)
                                    pe.wait_ge(dt_done, n - 1)
                                    if v < NLEV - 1:
                                        if v == 1 and u:
                                            pe.wait_ge(end_copied, 2 * (u - 1) + d + 1)
                                        for m in range(3):
                                            c = slice(m * P, (m + 1) * P)
                                            last = nc.tensor.matmul(psum[:, 4 + d, c], DT[:, d, c], X[:, d, c], start=True, stop=True)
                                        last.then_inc(d_prod, 1)
                                    for m in range(3):
                                        c = slice(m * P, (m + 1) * P)
                                        last = nc.tensor.matmul(psum[:, 6 + d, c], X[:, d, c], DT[:, d, c], start=True, stop=True)
                                    last.then_inc(dt_prod, 1)
                                if v == 1 and u + 1 < len(units):
                                    gate_rows(u + 1)
                                if v == 2 and u + 1 < len(units):
                                    products(u + 1)
                            for d in range(2):
                                pe.wait_ge(dt_done, (NLEV * (u + 1) - 1) * 2 + d + 1)
                                pe.wait_ge(kg_done, 2 * i + d + 1)
                                ph = slice(64 * par_, 64 * par_ + 64)
                                for m in range(3):
                                    h = 2 * m + par_
                                    c = slice(m * P, (m + 1) * P)
                                    nc.tensor.matmul(psum[:, 2 + d, m * HD:(m + 1) * HD], DT[:, d, c],
                                                     feat[:, i, (2 * GH + h) * HD:(2 * GH + h + 1) * HD], start=True, stop=True)
                                    last = nc.tensor.matmul(psum[ph, 4 + d, c], kg[:, d, h * HD:(h + 1) * HD], DT[:, d, c], start=True, stop=True)
                                last.then_inc(end_prod, 1)

                    @block.vector
                    def _(dve):
                        ch = Chain(dve, step)
                        ch(nc.vector.tensor_tensor(g[:, :, :], zb[:, :, B0 + H2:B0 + 2 * H2],
                                                   par(l, "dt_bias").unsqueeze(1).to_broadcast([P, NT, H2]), ALU.add))
                        dve.wait_ge(astep, 5)
                        ch(nc.vector.scalar_tensor_tensor(out=g[:, :, :], in0=g[:, :, :], scalar=0.0, in1=tmp[:, :, :], op0=ALU.max, op1=ALU.add))
                        nc.vector.scalar_tensor_tensor(out=g[:, :, :], in0=g[:, :, :], scalar=-1.0,
                                                       in1=na[:, :].unsqueeze(1).to_broadcast([P, NT, H2]),
                                                       op0=ALU.mult, op1=ALU.mult).then_inc(g_ready, 1)
                        dve.wait_ge(sums, 1)
                        for d in range(2):
                            ch(nc.vector.tensor_copy(gc[:, :, d * GH:(d + 1) * GH], psum[:, d, 0:NT * GH].rearrange("p (i h) -> p i h", h=GH)))
                        nc.vector.tensor_tensor(ek[:, :, :], psum[:, 4, 0:NT * H2].rearrange("p (i h) -> p i h", h=H2), gc[:, :, :],
                                                ALU.subtract).then_inc(gc_ready, 1)
                        dve.wait_ge(astep, 7)
                        nc.vector.tensor_tensor(ek[:, :, :], ek[:, :, :], beta[:, :, :], ALU.mult).then_inc(ek_ready, 1)

                        def differences(u):
                            i, par_ = units[u]
                            for d in range(2):
                                dve.wait_ge(rowed, 2 * u + d + 1)
                                for m in range(3):
                                    h = d * GH + 2 * m + par_
                                    c = slice(m * P, (m + 1) * P)
                                    last = nc.vector.tensor_scalar(E[:, d, c], psum[:, d, c], gc[:, i, h:h + 1], 0.0, ALU.subtract, ALU.min)
                                last.then_inc(dif_done, 1)

                        def decayed(u, d):
                            i, par_ = units[u]
                            dve.wait_ge(exp_done, 2 * u + d + 1)
                            for m in range(3):
                                h = d * GH + 2 * m + par_
                                c = slice(m * P, (m + 1) * P)
                                ch(nc.vector.scalar_tensor_tensor(out=E[:, d, c], in0=E[:, d, c], scalar=beta[:, i, h:h + 1],
                                                                  in1=cst("tri", d * P, (d + 1) * P), op0=ALU.mult, op1=ALU.mult))
                            dve.wait_ge(kk_done, u + 1)
                            for r in range(2):
                                ph = slice(64 * r, 64 * r + 64)
                                half = lambda ap: ap.rearrange("p (m n) -> p m n", n=P)[:, :, 64 * r:64 * r + 64]
                                dst = IT[ph, i, d].rearrange("p (m q n) -> p m q n", q=2, n=CHUNK)[:, :, par_]
                                ch(nc.vector.tensor_tensor(dst, half(psum[ph, 1, 0:3 * P]), half(E[ph, d]), ALU.mult))
                            nc.vector.tensor_tensor(LT[u % 2][:, d], psum[:, 0, 0:3 * P], E[:, d], ALU.mult).then_inc(lt_done, 1)

                        differences(0)
                        decayed(0, 0)
                        decayed(0, 1)
                        for u in range(len(units)):
                            for d in range(2):
                                if u:
                                    dve.wait_ge(end_prod, 2 * (u - 1) + d + 1)
                                lo = (1 - d) * NLEV * P
                                dve.wait_ge(lt_done, 2 * u + d + 1)
                                ch(nc.vector.tensor_tensor(v3(DT[:, d]), v3(LT[u % 2][:, d]), b3(cst("level", lo, lo + P)), ALU.mult))
                                nc.vector.tensor_tensor(v3(DT[:, d]), b3(cst("ident")), v3(DT[:, d]), ALU.subtract).then_inc(dt_done, 1)
                            for v in range(NLEV):
                                for d in range(2):
                                    n = (NLEV * u + v) * 2 + d
                                    dve.wait_ge(x_prod, n + 1)
                                    before = (NLEV - 1) * u + (v - 1 if v else 0)
                                    if before and v != 1:
                                        dve.wait_ge(dt_prod, 2 * (before - 1) + d + 1)
                                    lo = (d * NLEV + v) * P
                                    nc.vector.tensor_tensor(v3(X[:, d]), v3(psum[:, 2 + d, 0:3 * P]), b3(cst("level", lo, lo + P)),
                                                            ALU.mult).then_inc(x_done, 1)
                                if u + 1 < len(units):
                                    if v == 2:
                                        differences(u + 1)
                                    if v in (3, 4):
                                        decayed(u + 1, v - 3)
                                for d in range(2):
                                    n = (NLEV * u + v) * 2 + d
                                    if v < NLEV - 1:
                                        k = (NLEV - 1) * 2 * u + 2 * v + d
                                        if v:
                                            dve.wait_ge(d_prod, (NLEV - 2) * 2 * u + 2 * (v - 1) + d + 1)
                                            nc.vector.tensor_tensor(DD[:, d], DD[:, d], psum[:, 4 + d, 0:3 * P], ALU.subtract).then_inc(d_done, 1)
                                        else:
                                            dve.wait_ge(x_done, n + 1)
                                            nc.vector.tensor_tensor(v3(DD[:, d]), b3(cst("ident")), v3(X[:, d]), ALU.subtract).then_inc(d_done, 1)
                                    if v:
                                        dve.wait_ge(dt_prod, (NLEV - 1) * 2 * u + 2 * (v - 1) + d + 1)
                                        nc.vector.tensor_tensor(DT[:, d], DT[:, d], psum[:, 6 + d, 0:3 * P], ALU.subtract).then_inc(dt_done, 1)
                                    dve.wait_ge(dt_done, n + 1 if v else 2 * NLEV * u + 2)
                                    if v < NLEV - 1:
                                        dve.wait_ge(d_done, k + 1)
                S.end()

        def phase_gdn_scan(l, nq, U, WT, QT, IT, KO, gS, ob):
            NCC, NCL = CTXN // CHUNK, SEQ // CHUNK
            orders = [list(range(NCL, NCL + NCC)) + list(range(NCL)),
                      list(range(NCL + NCC - 1, NCL - 1, -1)) + list(range(NCL - 1, -1, -1))]
            items = [(t, d, orders[d][t]) for t in range(NCC + NCL) for d in range(2)]
            want = lambda c: c // 2 < nq
            st, S = ExitStack(), Sems(nc, f"gs{l}")
            with st:
                state = sbuf(st, "state", [P, 2, 3 * HD])
                decayed = sbuf(st, "decayed", [P, 2, 3 * HD])
                vn = sbuf(st, "vn", [P, 2, GH * HD])
                step, zeroed, ws_done, vn_done, sv_done, s_done, o_done = (
                    S("step"), S("zeroed"), S("ws_done"), S("vn_done"), S("sv_done"), S("s_done"), S("o_done"))
                hq = lambda ap: ap.rearrange("p (m q e) -> p q m e", q=2, e=HD)
                with nc.Block() as block:
                    @block.gpsimd
                    def _(pool):
                        nc.gpsimd.memset(state[:, :, :], 0.0).then_inc(zeroed, 1)
                        nc.gpsimd.memset(ob[:, :, :], 0.0).then_inc(zeroed, 1)

                    @block.tensor
                    def _(pe):
                        pe.wait_ge(zeroed, 2)

                        def first(k):
                            t, d, c = items[k]
                            i, r = c // 2, c % 2
                            R = slice(64 * r, 64 * r + 64)
                            if k >= 2:
                                pe.wait_ge(s_done, k - 1)
                                pe.wait_ge(o_done, k - 1)
                            for q in range(2):
                                ph = slice(64 * q, 64 * q + 64)
                                for m in range(3):
                                    sm = state[ph, d, m * HD:(m + 1) * HD]
                                    col = slice(m * P + 64 * r, m * P + 64 * r + 64)
                                    last = nc.tensor.matmul(psum[R, 4 * d + q, m * HD:(m + 1) * HD], WT[ph, i, d, col], sm, start=True, stop=True)
                                    if want(c):
                                        last = nc.tensor.matmul(psum[R, 4 * d + q, (3 + m) * HD:(4 + m) * HD], QT[ph, i, d, col], sm,
                                                                start=True, stop=True)
                            last.then_inc(ws_done, 1)

                        def second(k):
                            t, d, c = items[k]
                            i, r = c // 2, c % 2
                            R = slice(64 * r, 64 * r + 64)
                            pe.wait_ge(vn_done, k + 1)
                            for h in range(GH):
                                m, q = h // 2, h % 2
                                ph = slice(64 * q, 64 * q + 64)
                                v = vn[R, d, h * HD:(h + 1) * HD]
                                last = nc.tensor.matmul(psum[ph, 4 * d + 3, m * HD:(m + 1) * HD], KO[R, i, d, h * HD:(h + 1) * HD], v,
                                                        start=True, stop=True)
                            for h in range(GH):
                                v = vn[R, d, h * HD:(h + 1) * HD]
                                if want(c):
                                    last = nc.tensor.matmul(psum[R, 4 * d + 2, h * HD:(h + 1) * HD], IT[R, i, d, h * CHUNK:(h + 1) * CHUNK], v,
                                                            start=True, stop=True)
                            last.then_inc(sv_done, 1)

                        first(0)
                        for k in range(len(items)):
                            if k + 1 < len(items):
                                first(k + 1)
                            second(k)

                    @block.vector
                    def _(dve):
                        ch = Chain(dve, step)
                        dve.wait_ge(zeroed, 2)

                        def new_values(k):
                            t, d, c = items[k]
                            i, r = c // 2, c % 2
                            R = slice(64 * r, 64 * r + 64)
                            dve.wait_ge(ws_done, k + 1)
                            nc.vector.tensor_tensor(hq(vn[R, d]), hq(U[R, i, d]),
                                                    psum[R, 4 * d:4 * d + 2, 0:3 * HD].rearrange("p q (m e) -> p q m e", e=HD),
                                                    ALU.subtract).then_inc(vn_done, 1)
                            ch(nc.vector.tensor_tensor(decayed[:, d].rearrange("p (m e) -> p m e", e=HD),
                                                       state[:, d].rearrange("p (m e) -> p m e", e=HD),
                                                       gS[:, i, r, d].unsqueeze(2).to_broadcast([P, 3, HD]), ALU.mult))
                            if want(c):
                                o = hq(ob[R, i])
                                ch(nc.vector.tensor_tensor(o, o, psum[R, 4 * d:4 * d + 2, 3 * HD:6 * HD].rearrange("p q (m e) -> p q m e", e=HD), ALU.add))

                        def update(k):
                            t, d, c = items[k]
                            i, r = c // 2, c % 2
                            R = slice(64 * r, 64 * r + 64)
                            dve.wait_ge(sv_done, k + 1)
                            nc.vector.tensor_tensor(state[:, d], decayed[:, d], psum[:, 4 * d + 3, 0:3 * HD], ALU.add).then_inc(s_done, 1)
                            if want(c):
                                nc.vector.tensor_tensor(ob[R, i], ob[R, i], psum[R, 4 * d + 2, 0:GH * HD], ALU.add).then_inc(o_done, 1)
                            else:
                                dve.wait_ge(s_done, k + 1)
                                nc.vector.tensor_copy(decayed[:, d, 0:2], state[:, d, 0:2]).then_inc(o_done, 1)
                            dve.wait_ge(s_done, k + 1)
                            dve.wait_ge(o_done, k + 1)

                        new_values(0)
                        for k in range(len(items)):
                            if k + 1 < len(items):
                                new_values(k + 1)
                            update(k)
                S.end()

        def phase_merge(l, nq, zb, ob, score):
            st, S = ExitStack(), Sems(nc, f"mg{l}")
            GW = GH * HD
            with st:
                rows = sbuf(st, "rows2", [P, 3, 2, D])
                make_rows(l, "b", [(2, "mix_post", False), (4, "ffn_pre", True), (3, None, False)], rows)
                wo = sbuf(st, "wo", [P, DK, D])
                wr = sbuf(st, "wr", [P, DK, NE])
                ct = sbuf(st, "ct", [P, 2, D])
                xt = sbuf(st, "xt2", [P, 3, D])
                cT = sbuf(st, "cT2", [P, 2, D])
                tt = sbuf(st, "tt", [P, D])
                hh = sbuf(st, "hh2", [P, 2, D])
                hT = sbuf(st, "hT2", [P, 2, D])
                sq = sbuf(st, "sqm", [P, 2, GW])
                sz = sbuf(st, "sz", [P, 2, GW])
                junk = sbuf(st, "junk2", [P, 2, D])
                r1 = sbuf(st, "r1", [P, NT, GH])
                r2 = sbuf(st, "r2", [P, NT, 1])
                r3 = sbuf(st, "r3", [P, NT, 1])
                mh = sbuf(st, "mh4", [P, GH])
                w_in, wr_in = S("w_in"), S("wr_in")
                x_in, c_in = [S(f"x_in{r}") for r in range(3)], [S("c_in0"), S("c_in1")]
                gate_done, ms1, p1, cat_ready, turned_a, cT_ready, y_prod = (
                    S("gate_done"), S("ms1"), S("p1"), S("cat_ready"), S("turned_a"), S("cT_ready"), S("y_prod"))
                ssy_done, ms2, p2, x_ready, ssx_done, ms3, p3, h_ready = (
                    S("ssy_done"), S("ms2"), S("p2"), S("x_ready"), S("ssx_done"), S("ms3"), S("p3"), S("h_ready"))
                turned_c, hT_ready, lg_prod, score_done, step, astep, mh_set = (
                    S("turned_c"), S("hT_ready"), S("lg_prod"), S("score_done"), S("step"), S("astep"), S("mh_set"))
                x_out, h_out = [S(f"x_out{r}") for r in range(3)], [S("h_out0"), S("h_out1")]

                def skewed(a, b, c):
                    for s in range(nq + 2):
                        if 0 <= s - 2 < nq:
                            c(s - 2)
                        if 0 <= s - 1 < nq:
                            b(s - 1)
                        if s < nq:
                            a(s)

                with nc.Block() as block:
                    @block.sync
                    def _(sp):
                        def load(i):
                            if i >= 2:
                                sp.wait_ge(turned_a, i - 1)
                            if i >= 3:
                                sp.wait_ge(x_out[i % 3], 16 * (i // 3))
                                sp.wait_ge(h_ready, i - 2)
                                sp.wait_ge(ssx_done, i - 2)
                            for a, b in ((0, SWA_H * HD), ((SWA_H + GH) * HD, D)):
                                sp.dma_start(ct[:, i % 2, a:b], cat_dram[i * P:(i + 1) * P, a:b]).then_inc(c_in[i % 2], 16)
                            sp.dma_start(xt[:, i % 3], xres[i * P:(i + 1) * P, :]).then_inc(x_in[i % 3], 16)

                        load(0)
                        sp.dma_start(wo[:, :, :], A["w_out"][l]).then_inc(w_in, 16)
                        load(1)
                        sp.dma_start(wr[:, :, :], A["router"][l]).then_inc(wr_in, 16)
                        if nq > 2:
                            load(2)
                        for i in range(nq):
                            sp.wait_ge(x_ready, i + 1)
                            sp.dma_start(xres[i * P:(i + 1) * P, :], xt[:, i % 3]).then_inc(x_out[i % 3], 16)
                            sp.wait_ge(h_ready, i + 1)
                            sp.dma_start(h2_dram[i * P:(i + 1) * P, :], hh[:, i % 2]).then_inc(h_out[i % 2], 16)
                            if i + 3 < nq:
                                load(i + 3)
                        for r in range(3):
                            sp.wait_ge(x_out[r], 16 * len(range(r, nq, 3)))
                        for r in range(2):
                            sp.wait_ge(h_out[r], 16 * len(range(r, nq, 2)))

                    @block.gpsimd
                    def _(pool):
                        nc.gpsimd.memset(mh[:, :], -0.5).then_inc(mh_set, 1)
                        pool.wait_ge(mh_set, 1)

                        def power(wait, r, sem):
                            def f(i):
                                pool.wait_ge(wait, i + 1)
                                nc.gpsimd.tensor_tensor(r[:, i], r[:, i], mh[:, 0:r.shape[2]], ALU.pow).then_inc(sem, 1)
                            return f

                        b2, b3_ = power(ms2, r2, p2), power(ms3, r3, p3)

                        def b(i):
                            b2(i)
                            b3_(i)
                        skewed(power(ms1, r1, p1), b, lambda i: None)

                    @block.scalar
                    def _(act):
                        ch = Chain(act, astep)

                        def a(i):
                            if i >= 2:
                                act.wait_ge(cat_ready, i - 1)
                            nc.scalar.activation(sq[:, i % 2], ob[:, i], ACT.Square)
                            nc.scalar.activation(sz[:, i % 2], zb[:, i, 0:GW], ACT.Silu).then_inc(gate_done, 1)
                            act.wait_ge(turned_a, i + 1)
                            if i >= 2:
                                act.wait_ge(y_prod, i - 1)
                            nc.scalar.copy(cT[:, i % 2].rearrange("p (b n) -> p b n", b=2), psum[:, 0:2, :]).then_inc(cT_ready, 1)

                        def b(i):
                            act.wait_ge(y_prod, i + 1)
                            if i:
                                act.wait_ge(ssx_done, i)
                            nc.scalar.activation(junk[:, 0].rearrange("p (b n) -> p b n", b=2), psum[:, 2:4, :], ACT.Square, accum_out=r2[:, i]).then_inc(ssy_done, 1)
                            act.wait_ge(x_ready, i + 1)
                            nc.scalar.activation(junk[:, 1], xt[:, i % 3], ACT.Square, accum_out=r3[:, i]).then_inc(ssx_done, 1)

                        def c(i):
                            act.wait_ge(turned_c, i + 1)
                            if i >= 2:
                                act.wait_ge(lg_prod, i - 1)
                            nc.scalar.copy(hT[:, i % 2].rearrange("p (b n) -> p b n", b=2), psum[:, 4:6, :]).then_inc(hT_ready, 1)
                            act.wait_ge(lg_prod, i + 1)
                            nc.scalar.activation(score[:, i], psum[:, 6 + i % 2, 0:NE], ACT.Sigmoid).then_inc(score_done, 1)

                        skewed(a, b, c)

                    @block.tensor
                    def _(pe):
                        def turn(src, bank):
                            for k in range(DK):
                                last = nc.tensor.transpose(psum[:, bank + k // 4, (k % 4) * P:(k % 4 + 1) * P],
                                                           src[:, k * P:(k + 1) * P], cst("ident"))
                            return last

                        def a(i):
                            pe.wait_ge(cat_ready, i + 1)
                            if i:
                                pe.wait_ge(cT_ready, i)
                            turn(ct[:, i % 2], 0).then_inc(turned_a, 1)

                        def b(i):
                            if i == 0:
                                pe.wait_ge(w_in, 16)
                            pe.wait_ge(cT_ready, i + 1)
                            if i:
                                pe.wait_ge(x_ready, i)
                            for n in range(2):
                                for k in range(DK):
                                    last = nc.tensor.matmul(psum[:, 2 + n, :], cT[:, i % 2, k * P:(k + 1) * P],
                                                            wo[:, k, n * 512:(n + 1) * 512], start=(k == 0), stop=(k == DK - 1))
                            last.then_inc(y_prod, 1)

                        def c(i):
                            if i == 0:
                                pe.wait_ge(wr_in, 16)
                            pe.wait_ge(h_ready, i + 1)
                            turn(hh[:, i % 2], 4).then_inc(turned_c, 1)
                            pe.wait_ge(hT_ready, i + 1)
                            if i >= 2:
                                pe.wait_ge(score_done, i - 1)
                            for k in range(DK):
                                last = nc.tensor.matmul(psum[:, 6 + i % 2, 0:NE], hT[:, i % 2, k * P:(k + 1) * P], wr[:, k, :],
                                                        start=(k == 0), stop=(k == DK - 1))
                            last.then_inc(lg_prod, 1)

                        skewed(a, b, c)

                    @block.vector
                    def _(dve):
                        ch = Chain(dve, step)
                        hv = lambda ap: ap.rearrange("p (h e) -> p h e", e=HD)

                        def a(i):
                            dve.wait_ge(gate_done, i + 1)
                            ch(nc.vector.tensor_reduce(r1[:, i], hv(sq[:, i % 2]), AX.X, ALU.add))
                            nc.vector.tensor_scalar(r1[:, i], r1[:, i], 1.0 / HD, EPS, ALU.mult, ALU.add).then_inc(ms1, 1)
                            dve.wait_ge(c_in[i % 2], 32 * (i // 2) + 32)
                            if i >= 2:
                                dve.wait_ge(turned_a, i - 1)
                            ch(nc.vector.tensor_tensor(hv(sz[:, i % 2]), hv(sz[:, i % 2]),
                                                       par(l, "gdn_norm").unsqueeze(1).to_broadcast([P, GH, HD]), ALU.mult))
                            ch(nc.vector.tensor_tensor(sz[:, i % 2], sz[:, i % 2], ob[:, i], ALU.mult))
                            dve.wait_ge(p1, i + 1)
                            nc.vector.tensor_tensor(hv(ct[:, i % 2, SWA_H * HD:(SWA_H + GH) * HD]), hv(sz[:, i % 2]),
                                                    r1[:, i].unsqueeze(2).to_broadcast([P, GH, HD]), ALU.mult).then_inc(cat_ready, 1)

                        def b(i):
                            s = 0 if i < NLT else 1
                            dve.wait_ge(ssy_done, i + 1)
                            nc.vector.tensor_scalar(r2[:, i], r2[:, i], 1.0 / D, EPS, ALU.mult, ALU.add).then_inc(ms2, 1)
                            dve.wait_ge(p2, i + 1)
                            b2 = lambda ap: ap.rearrange("p (b n) -> p b n", b=2)
                            ch(nc.vector.scalar_tensor_tensor(out=b2(tt[:, :]), in0=psum[:, 2:4, :], scalar=r2[:, i],
                                                              in1=b2(rows[:, 0, s]), op0=ALU.mult, op1=ALU.mult))
                            dve.wait_ge(x_in[i % 3], 16 * (i // 3) + 16)
                            nc.vector.tensor_tensor(xt[:, i % 3], xt[:, i % 3], tt[:, :], ALU.add).then_inc(x_ready, 1)
                            dve.wait_ge(ssx_done, i + 1)
                            nc.vector.tensor_scalar(r3[:, i], r3[:, i], 1.0 / D, EPS, ALU.mult, ALU.add).then_inc(ms3, 1)
                            dve.wait_ge(p3, i + 1)
                            if i >= 2:
                                dve.wait_ge(turned_c, i - 1)
                                dve.wait_ge(h_out[i % 2], 16 * (i // 2))
                            ch(nc.vector.scalar_tensor_tensor(out=hh[:, i % 2], in0=xt[:, i % 3], scalar=r3[:, i],
                                                              in1=rows[:, 1, s], op0=ALU.mult, op1=ALU.mult))
                            nc.vector.tensor_tensor(hh[:, i % 2], hh[:, i % 2], rows[:, 2, s], ALU.add).then_inc(h_ready, 1)

                        skewed(a, b, lambda i: None)
                S.end()

        def phase_route(l, nq, score, dest, wk, idx, bexp):
            st, S = ExitStack(), Sems(nc, f"rt{l}")
            NB = nq + nq * TOPK + NE
            NBC = NB + 1
            with st:
                sel = sbuf(st, "sel", [P, nq, NE])
                g8 = sbuf(st, "g8", [P, nq, NGRP, 8])
                gs = sbuf(st, "gs", [P, nq, NGRP])
                c1 = sbuf(st, "c1", [P, nq, NGRP, NGRP])
                c2 = sbuf(st, "c2", [P, nq, NGRP, NGRP])
                rank = sbuf(st, "rank", [P, nq, NGRP])
                m8 = sbuf(st, "m8", [P, nq, 8])
                M = sbuf(st, "M", [P, nq, NE])
                wn = sbuf(st, "wn", [P, nq, NE])
                ws = sbuf(st, "ws", [P, nq])
                nblk = sbuf(st, "nblk", [P, NE])
                ends = sbuf(st, "ends", [P, NE])
                tmpe = sbuf(st, "tmpe", [P, NE])
                d8 = sbuf(st, "d8", [P, nq, 8])
                big = sbuf(st, "bigr", [P, 8, NE])
                cmpb = sbuf(st, "cmpb", [NE, P])
                bf = sbuf(st, "bf", [1, NBC + 2])
                tab = sbuf(st, "tab", [P, NBC], I32)
                toki = sbuf(st, "toki", [P, NT], I32)
                di = sbuf(st, "di", [P, nq, 8], I32)
                sidx = sbuf(st, "sidx", [P, nq, 8], I32)
                step, m_ready, pos_done, ends_ready, col_done, cmp_ready, be_done = (
                    S("step"), S("m_ready"), S("pos_done"), S("ends_ready"), S("col_done"), S("cmp_ready"), S("be_done"))
                tab_ready, tab_out, sidx_ready, scattered, idx_in = S("tab_ready"), S("tab_out"), S("sidx_ready"), S("scattered"), S("idx_in")
                tab_dram = nc.dram_tensor(f"slot_tokens{l}", (P * NBC, 1), I32).ap()
                with nc.Block() as block:
                    @block.vector
                    def _(dve):
                        ch = Chain(dve, step)
                        V = nc.vector
                        ch(V.memset(tab[:, :], 0))
                        ch(V.tensor_copy(toki[:, :], cst("tokid")))
                        V.tensor_copy(tab[:, 0:nq], cst("tokid", 0, nq)).then_inc(tab_ready, 1)
                        ch(V.tensor_tensor(sel[:, :, :], score[:, :, :], par(l, "router_bias").unsqueeze(1).to_broadcast([P, nq, NE]), ALU.add))
                        for i in range(nq):
                            for q in range(NGRP):
                                ch(V.max(out=g8[:, i, q], in_=sel[:, i, q * GSZ:(q + 1) * GSZ]))
                        ch(V.tensor_tensor(gs[:, :, :], g8[:, :, :, 0], g8[:, :, :, 1], ALU.add))
                        other = gs[:, :, :].unsqueeze(2).to_broadcast([P, nq, NGRP, NGRP])
                        own = gs[:, :, :].unsqueeze(3).to_broadcast([P, nq, NGRP, NGRP])
                        ch(V.tensor_tensor(c1[:, :, :, :], other, own, ALU.is_gt))
                        ch(V.tensor_tensor(c2[:, :, :, :], other, own, ALU.is_equal))
                        ch(V.tensor_tensor(c2[:, :, :, :].rearrange("p i a b -> p i (a b)"), c2[:, :, :, :].rearrange("p i a b -> p i (a b)"),
                                           cst("gcmp").unsqueeze(1).to_broadcast([P, nq, NGRP * NGRP]), ALU.mult))
                        ch(V.tensor_tensor(c1[:, :, :, :], c1[:, :, :, :], c2[:, :, :, :], ALU.add))
                        ch(V.tensor_reduce(rank[:, :, :], c1[:, :, :, :], AX.X, ALU.add))
                        ch(V.tensor_scalar(rank[:, :, :], rank[:, :, :], TOPG - 0.5, None, ALU.is_lt))
                        ch(V.tensor_scalar(rank[:, :, :], rank[:, :, :], BIG, -BIG, ALU.mult, ALU.add))
                        grp = lambda ap: ap.rearrange("p i (g e) -> p i g e", g=NGRP)
                        ch(V.tensor_tensor(grp(sel[:, :, :]), grp(sel[:, :, :]), rank[:, :, :].unsqueeze(3).to_broadcast([P, nq, NGRP, GSZ]), ALU.add))
                        for i in range(nq):
                            ch(V.max(out=m8[:, i], in_=sel[:, i]))
                            ch(V.match_replace(out=wn[:, i], in_to_replace=m8[:, i], in_values=sel[:, i], imm_value=-3 * BIG))
                        V.tensor_scalar(M[:, :, :], wn[:, :, :], -2 * BIG, None, ALU.is_lt).then_inc(m_ready, 1)
                        dve.wait_ge(m_ready, 1)
                        ch(V.tensor_tensor(wn[:, :, :], score[:, :, :], M[:, :, :], ALU.mult))
                        ch(V.tensor_reduce(ws[:, :], wn[:, :, :], AX.X, ALU.add))
                        ch(V.reciprocal(ws[:, :], ws[:, :]))
                        ch(V.tensor_scalar(ws[:, :], ws[:, :], ROUTED_SCALE, None, ALU.mult))
                        ch(V.tensor_tensor(wn[:, :, :], wn[:, :, :], ws[:, :].unsqueeze(2).to_broadcast([P, nq, NE]), ALU.mult))
                        dve.wait_ge(pos_done, 1)
                        cnt = psum[:, 1, 0:NE]
                        ch(V.tensor_scalar(nblk[:, :], cnt, 0.5, None, ALU.is_gt))
                        for j in range(1, nq):
                            ch(V.scalar_tensor_tensor(out=nblk[:, :], in0=cnt, scalar=j * P + 0.5, in1=nblk[:, :], op0=ALU.is_gt, op1=ALU.add))
                        ch(V.memset(tmpe[:, :], 1.0))
                        V.tensor_tensor_scan(ends[:, :], tmpe[:, :], nblk[:, :], 0.0, ALU.mult, ALU.add).then_inc(ends_ready, 1)
                        dve.wait_ge(ends_ready, 1)
                        ch(V.tensor_tensor(tmpe[:, :], ends[:, :], nblk[:, :], ALU.subtract))
                        ch(V.tensor_scalar(tmpe[:, :], tmpe[:, :], float(P), nq * P + 1.0, ALU.mult, ALU.add))
                        pos = psum[:, 0, 0:nq * NE].rearrange("p (i e) -> p i e", e=NE)
                        ch(V.tensor_tensor(sel[:, :, :], pos, tmpe[:, :].unsqueeze(1).to_broadcast([P, nq, NE]), ALU.add))
                        ch(V.tensor_tensor(sel[:, :, :], sel[:, :, :], M[:, :, :], ALU.mult))
                        for i in range(nq):
                            ch(V.max(out=d8[:, i], in_=sel[:, i]))
                        ch(V.tensor_scalar(m8[:, :, :], d8[:, :, :], -1.0, None, ALU.add))
                        ch(V.tensor_copy(di[:, :, :], m8[:, :, :]))
                        ch(V.tensor_copy(dest[:, :, :], di[:, :, :]))
                        ch(V.tensor_scalar(sidx[:, :, :], di[:, :, :], P - 1, None, ALU.bitwise_and))
                        ch(V.tensor_scalar(di[:, :, :], di[:, :, :], 7, None, ALU.logical_shift_right))
                        ch(V.tensor_copy(m8[:, :, :], sidx[:, :, :]))
                        ch(V.tensor_scalar(m8[:, :, :], m8[:, :, :], float(NBC), None, ALU.mult))
                        ch(V.tensor_tensor(m8[:, :, :], m8[:, :, :], di[:, :, :], ALU.add))
                        V.tensor_copy(sidx[:, :, :], m8[:, :, :]).then_inc(sidx_ready, 1)
                        dve.wait_ge(col_done, 1)
                        ch(V.tensor_copy(big[0:NE, 0, 0:1], psum[0:NE, 2, 0:1]))
                        ch(V.tensor_scalar(big[0:NE, 0, 0:1], big[0:NE, 0, 0:1], float(nq), None, ALU.add))
                        V.tensor_scalar(cmpb[:, :], cst("iota")[0:NE], big[0:NE, 0, 0:1], None, ALU.is_ge).then_inc(cmp_ready, 1)
                        dve.wait_ge(be_done, 1)
                        ch(V.tensor_copy(bf[:, 0:NB], psum[0:1, 3, 0:NB]))
                        ch(V.memset(bf[:, 0:nq], float(NE)))
                        ch(V.memset(bf[:, NB:NBC + 1], 0.0))
                        ch(V.tensor_scalar(bf[:, NBC + 1:NBC + 2], ends[0:1, NE - 1:NE], float(nq), None, ALU.add))
                        ch(V.tensor_copy(bexp[:, 0:NBC + 2], bf[:, :]))
                        ch(V.tensor_scalar(bf[:, NBC:NBC + 1], bf[:, NBC + 1:NBC + 2], 1.0, None, ALU.add))
                        ch(V.tensor_copy(bexp[:, NBC + 2:NBC + 3], bf[:, NBC:NBC + 1]))
                        ch(V.tensor_scalar(bexp[:, NBC + 2:NBC + 3], bexp[:, NBC + 2:NBC + 3], 1, None, ALU.logical_shift_right))
                        for i in range(nq):
                            ch(V.tensor_tensor(big[:, :, :], sel[:, i].unsqueeze(1).to_broadcast([P, 8, NE]),
                                               d8[:, i].unsqueeze(2).to_broadcast([P, 8, NE]), ALU.is_equal))
                            ch(V.tensor_tensor(big[:, :, :], big[:, :, :], wn[:, i].unsqueeze(1).to_broadcast([P, 8, NE]), ALU.mult))
                            ch(V.tensor_reduce(wk[:, i], big[:, :, :], AX.X, ALU.add))

                    @block.tensor
                    def _(pe):
                        pe.wait_ge(m_ready, 1)
                        for i in range(nq):
                            for j in range(i + 1):
                                nc.tensor.matmul(psum[:, 0, i * NE:(i + 1) * NE], cst("before") if j == i else cst("ones"), M[:, j],
                                                 start=(j == 0), stop=(j == i))
                        for j in range(nq):
                            last = nc.tensor.matmul(psum[:, 1, 0:NE], cst("ones"), M[:, j], start=(j == 0), stop=(j == nq - 1))
                        last.then_inc(pos_done, 1)
                        pe.wait_ge(ends_ready, 1)
                        nc.tensor.matmul(psum[0:NE, 2, 0:1], ends[0:1, :], cst("ones")[0:1, 0:1], start=True, stop=True).then_inc(col_done, 1)
                        pe.wait_ge(cmp_ready, 1)
                        nc.tensor.matmul(psum[0:1, 3, 0:P], cst("ones")[0:NE, 0:1], cmpb[:, :], start=True, stop=True).then_inc(be_done, 1)

                    @block.sync
                    def _(sp):
                        sp.wait_ge(tab_ready, 1)
                        sp.dma_start(tab_dram.rearrange("(p n) o -> p (n o)", n=NBC), tab[:, :]).then_inc(tab_out, 16)
                        sp.wait_ge(scattered, 16 * nq * TOPK)
                        sp.dma_start(idx[:, 0:NBC], tab_dram.rearrange("(p n) o -> p (n o)", n=NBC)).then_inc(idx_in, 16)
                        sp.wait_ge(idx_in, 16)

                    @block.gpsimd
                    def _(pool):
                        pool.wait_ge(tab_out, 16)
                        pool.wait_ge(sidx_ready, 1)
                        for i in range(nq):
                            for k in range(TOPK):
                                nc.gpsimd.indirect_dma_start(tab_dram, bass.IndirectOffsetOnAxis(ap=sidx[:, i, k:k + 1], axis=0),
                                                             toki[:, i:i + 1], None).then_inc(scattered, 16)
                        pool.wait_ge(scattered, 16 * nq * TOPK)
                S.end()

        def phase_experts(l, nq, idx, bexp):
            NB = nq + nq * TOPK + NE
            st, S = ExitStack(), Sems(nc, f"ex{l}")
            with st:
                wgu = sbuf(st, "wgu", [P, 2, DK, 2 * DE])
                wdn = sbuf(st, "wdn", [P, 2, 2, D])
                xg = sbuf(st, "xg", [P, 2, D])
                xT = sbuf(st, "xTe", [P, 2, D])
                sg = sbuf(st, "sg", [P, 2, DE])
                hid = sbuf(st, "hid", [P, 2, DE])
                hT = sbuf(st, "hTe", [P, 2, DE])
                yb = sbuf(st, "yb", [P, 2, D])
                w_in, gathered, y_out = [S("w_in0"), S("w_in1")], [S("gathered0"), S("gathered1")], [S("y_out0"), S("y_out1")]
                turned, xT_ready, gu_done, silu_done, hid_ready = (
                    S("turned"), S("xT_ready"), S("gu_done"), S("silu_done"), S("hid_ready"))
                hturned, hT_ready, down_done, yv_ready, ys_ready = S("hturned"), S("hT_ready"), S("down_done"), S("yv_ready"), S("ys_ready")
                stores_done = S("stores_done")

                def used_pairs(eng):
                    return eng.value_load(bexp[0:1, NB + 3:NB + 4], min_val=0, max_val=NB // 2)

                with nc.Block() as block:
                    @block.sync
                    def _(sp):
                        total = sp.value_load(bexp[0:1, NB + 2:NB + 3], min_val=0, max_val=NB)
                        pairs = used_pairs(sp)

                        def load(b, r, always=False):
                            e = sp.value_load(bexp[0:1, bass.ds(b, 1)], min_val=0, max_val=NE)
                            kw = {} if always else {"cond": total > b}
                            sp.dma_start(wgu[:, r].rearrange("p k n -> p (k n)"),
                                         A["w_gu"][bass.ds(e + l * (NE + 1), 1)].rearrange("e p k n -> (e p) (k n)"), **kw).then_inc(w_in[r], 16)
                            sp.dma_start(wdn[:, r].rearrange("p k n -> p (k n)"),
                                         A["w_dn"][bass.ds(e + l * (NE + 1), 1)].rearrange("e p k n -> (e p) (k n)"), **kw).then_inc(w_in[r], 16)

                        def store(b, r):
                            sp.dma_start(y_dram[bass.ds(b * P, P), :], yb[:, r]).then_inc(y_out[r], 16)

                        load(0, 0, True)
                        load(1, 1, True)
                        with sp.Fori(0, NB // 2) as i:
                            with sp.If(pairs > i):
                                for r in range(2):
                                    b = 2 * i + r
                                    sp.wait_ge(down_done, b + 1)
                                    load(b + 2, r)
                                    sp.wait_ge(yv_ready, b + 2)
                                    sp.wait_ge(ys_ready, b + 2)
                                    store(b, r)
                        sp.wait_ge(stores_done, 2)

                    @block.gpsimd
                    def _(pool):
                        pairs = used_pairs(pool)

                        def gather(b):
                            if b >= 2:
                                pool.wait_ge(turned, b - 1)
                            nc.gpsimd.indirect_dma_start(xg[:, b % 2], None, h2_dram,
                                                         bass.IndirectOffsetOnAxis(ap=idx[:, b:b + 1], axis=0)
                                                         ).then_inc(gathered[b % 2], 16)

                        gather(0)
                        for j in range(NB // 2):
                            with pool.If(pairs > j):
                                gather(2 * j + 1)
                                gather(2 * j + 2)

                    @block.tensor
                    def _(pe):
                        def turn(r):
                            for k in range(DK):
                                last = nc.tensor.transpose(psum[:, k // 4, (k % 4) * P:(k % 4 + 1) * P],
                                                           xg[:, r, k * P:(k + 1) * P], cst("ident"))
                            last.then_inc(turned, 1)

                        pe.wait_ge(gathered[0], 16)
                        turn(0)
                        pairs = used_pairs(pe)
                        with pe.Fori(0, NB // 2) as i:
                            with pe.If(pairs > i):
                                for r in range(2):
                                    b = 2 * i + r
                                    pe.wait_ge(w_in[r], 32 * i + 32)
                                    pe.wait_ge(xT_ready, b + 1)
                                    pe.wait_ge(hid_ready, b + 1)
                                    for k in range(DK):
                                        last = nc.tensor.matmul(psum[:, 2 + r, :], xT[:, r, k * P:(k + 1) * P], wgu[:, r, k, :],
                                                                start=(k == 0), stop=(k == DK - 1))
                                    last.then_inc(gu_done, 1)
                                    pe.wait_ge(gathered[1 - r], 16 * i + 16 * (r + 1))
                                    turn(1 - r)
                                    pe.wait_ge(hid_ready, b + 3)
                                    for j in range(2):
                                        last = nc.tensor.transpose(psum[:, 4, j * P:(j + 1) * P], hid[:, r, j * P:(j + 1) * P], cst("ident"))
                                    last.then_inc(hturned, 1)
                                    pe.wait_ge(hT_ready, b + 1)
                                    pe.wait_ge(yv_ready, b + 1)
                                    pe.wait_ge(ys_ready, b + 1)
                                    for n in range(2):
                                        for j in range(2):
                                            last = nc.tensor.matmul(psum[:, 5 + n, :], hT[:, r, j * P:(j + 1) * P],
                                                                    wdn[:, r, j, n * 512:(n + 1) * 512], start=(j == 0), stop=(j == 1))
                                    last.then_inc(down_done, 1)

                    @block.scalar
                    def _(act):
                        def take_x(r):
                            nc.scalar.copy(xT[:, r].rearrange("p (b n) -> p b n", b=2), psum[:, 0:2, :]).then_inc(xT_ready, 1)

                        for r in range(2):
                            nc.scalar.activation(yb[:, r, 0:2], cst("ones", 0, 2), ACT.Copy).then_inc(y_out[r], 16)
                        act.wait_ge(y_out[0], 16)
                        nc.scalar.activation(yb[:, 0, 0:2], cst("ones", 0, 2), ACT.Copy).then_inc(ys_ready, 1)
                        act.wait_ge(turned, 1)
                        take_x(0)
                        pairs = used_pairs(act)
                        with act.Fori(0, NB // 2) as i:
                            with act.If(pairs > i):
                                for r in range(2):
                                    b = 2 * i + r
                                    act.wait_ge(gu_done, b + 1)
                                    nc.scalar.activation(sg[:, r], psum[:, 2 + r, 0:DE], ACT.Silu).then_inc(silu_done, 1)
                                    act.wait_ge(turned, b + 2)
                                    take_x(1 - r)
                                    act.wait_ge(down_done, b + 1)
                                    act.wait_ge(y_out[r], 16 * i + 16)
                                    nc.scalar.copy(yb[:, r, 0:512], psum[:, 5, :]).then_inc(ys_ready, 1)

                        for r in range(2):
                            act.wait_ge(w_in[r], 32 * pairs + 32)
                            act.wait_ge(y_out[r], 16 * pairs + 16)
                            nc.scalar.copy(sg[:, r, 0:2], yb[:, r, 0:2]).then_inc(stores_done, 1)

                    @block.vector
                    def _(dve):
                        for r in range(2):
                            nc.vector.memset(hid[:, r, :], 0.0).then_inc(hid_ready, 1)
                        nc.vector.memset(yb[:, 0, 512:514], 0.0).then_inc(yv_ready, 1)
                        dve.wait_ge(yv_ready, 1)
                        dve.wait_ge(hid_ready, 2)
                        pairs = used_pairs(dve)
                        with dve.Fori(0, NB // 2) as i:
                            with dve.If(pairs > i):
                                for r in range(2):
                                    b = 2 * i + r
                                    dve.wait_ge(silu_done, b + 1)
                                    nc.vector.tensor_tensor(hid[:, r], sg[:, r], psum[:, 2 + r, DE:2 * DE], ALU.mult).then_inc(hid_ready, 1)
                                    dve.wait_ge(hturned, b + 1)
                                    nc.vector.tensor_copy(hT[:, r], psum[:, 4, 0:DE]).then_inc(hT_ready, 1)
                                    dve.wait_ge(down_done, b + 1)
                                    dve.wait_ge(y_out[r], 16 * i + 16)
                                    nc.vector.tensor_copy(yb[:, r, 512:D], psum[:, 6, :]).then_inc(yv_ready, 1)
                S.end()

        def phase_combine(l, nq, dest, wk):
            NG = 6
            last_layer = l == NLAYER - 1
            st, S = ExitStack(), Sems(nc, f"cb{l}")
            with st:
                rows = sbuf(st, "rows3", [P, 1, 2, D])
                make_rows(l, "c", [(5, "ffn_post", False)], rows)
                G = sbuf(st, "G", [P, NG, D])
                sh = sbuf(st, "sh", [P, 2, D])
                xt = sbuf(st, "xt3", [P, 2, D])
                acc = sbuf(st, "acc2", [P, 2, D])
                junk = sbuf(st, "junk3", [P, D])
                rs = sbuf(st, "rs3", [P, NT])
                mh = sbuf(st, "mh5", [P, 1])
                gathered = [S(f"gathered{q}") for q in range(NG)]
                s_in, x_in, x_out = [S("s_in0"), S("s_in1")], [S("x_in0"), S("x_in1")], [S("x_out0"), S("x_out1")]
                step, used, ss_done, ms_done, rs_done, x_ready, mh_set = (
                    S("step"), S("used"), S("ss_done"), S("ms_done"), S("rs_done"), S("x_ready"), S("mh_set"))
                with nc.Block() as block:
                    @block.sync
                    def _(sp):
                        def load(i):
                            if i >= 2:
                                sp.wait_ge(used, TOPK * (i - 2) + 1)
                                sp.wait_ge(x_out[i % 2], 16 * (i // 2))
                            sp.dma_start(sh[:, i % 2], y_dram[i * P:(i + 1) * P, :]).then_inc(s_in[i % 2], 16)
                            sp.dma_start(xt[:, i % 2], xres[i * P:(i + 1) * P, :]).then_inc(x_in[i % 2], 16)

                        load(0)
                        load(1)
                        for i in range(nq):
                            sp.wait_ge(x_ready, i + 1)
                            dst = out[0, i * P:(i + 1) * P, :] if last_layer else xres[i * P:(i + 1) * P, :]
                            sp.dma_start(dst, xt[:, i % 2]).then_inc(x_out[i % 2], 16)
                            if i + 2 < nq:
                                load(i + 2)
                        for r in range(2):
                            sp.wait_ge(x_out[r], 16 * (nq // 2))

                    @block.gpsimd
                    def _(pool):
                        nc.gpsimd.memset(mh[:, :], -0.5).then_inc(mh_set, 1)
                        pool.wait_ge(mh_set, 1)

                        def power(i):
                            pool.wait_ge(ms_done, i + 1)
                            nc.gpsimd.tensor_tensor(rs[:, i:i + 1], rs[:, i:i + 1], mh[:, :], ALU.pow).then_inc(rs_done, 1)

                        for i in range(nq):
                            for k in range(TOPK):
                                n = i * TOPK + k
                                if n >= NG:
                                    pool.wait_ge(used, n - NG + 1)
                                nc.gpsimd.indirect_dma_start(G[:, n % NG], None, y_dram,
                                                             bass.IndirectOffsetOnAxis(ap=dest[:, i, k:k + 1], axis=0)
                                                             ).then_inc(gathered[n % NG], 16)
                                if k == NG - 1 and i:
                                    power(i - 1)
                        power(nq - 1)

                    @block.scalar
                    def _(act):
                        for i in range(nq):
                            act.wait_ge(used, TOPK * (i + 1))
                            if i:
                                act.wait_ge(ss_done, i)
                            nc.scalar.activation(junk[:, :], acc[:, i % 2], ACT.Square, accum_out=rs[:, i:i + 1]).then_inc(ss_done, 1)

                    @block.vector
                    def _(dve):
                        ch = Chain(dve, step)

                        def finish(i):
                            s = 0 if i < NLT else 1
                            dve.wait_ge(rs_done, i + 1)
                            ch(nc.vector.scalar_tensor_tensor(out=acc[:, i % 2], in0=acc[:, i % 2], scalar=rs[:, i:i + 1], in1=rows[:, 0, s],
                                                              op0=ALU.mult, op1=ALU.mult))
                            dve.wait_ge(x_in[i % 2], 16 * (i // 2) + 16)
                            nc.vector.tensor_tensor(xt[:, i % 2], xt[:, i % 2], acc[:, i % 2], ALU.add).then_inc(x_ready, 1)
                            dve.wait_ge(x_ready, i + 1)

                        for i in range(nq):
                            for k in range(TOPK):
                                n = i * TOPK + k
                                dve.wait_ge(gathered[n % NG], 16 * (n // NG) + 16)
                                if k == 0:
                                    dve.wait_ge(s_in[i % 2], 16 * (i // 2) + 16)
                                nc.vector.scalar_tensor_tensor(out=acc[:, i % 2], in0=G[:, n % NG], scalar=wk[:, i, k:k + 1],
                                                               in1=acc[:, i % 2] if k else sh[:, i % 2],
                                                               op0=ALU.mult, op1=ALU.add).then_inc(used, 1)
                                dve.wait_ge(used, n + 1)
                            dve.wait_ge(ss_done, i + 1)
                            nc.vector.tensor_scalar(rs[:, i:i + 1], rs[:, i:i + 1], 1.0 / D, EPS, ALU.mult, ALU.add).then_inc(ms_done, 1)
                            finish(i)
                S.end()

        def mixer(l, nq, zb, ob):
            keep, feats, att, conv = ExitStack(), ExitStack(), ExitStack(), ExitStack()
            with keep:
                with feats:
                    with att:
                        with conv:
                            chan = sbuf(conv, "chan", [P, NGT, CW])
                            patt = sbuf(att, "patt", [P, NT, W_ATT])
                            phase_project(l, patt, zb, chan)
                            feat = sbuf(feats, "feat", [P, NT, GCH])
                            gqT = sbuf(feats, "gqT", [P, 3, NTOK])
                            gkT = sbuf(feats, "gkT", [P, 3, NTOK])
                            phase_gdn_features(l, chan, feat, gqT, gkT)
                        sqT = sbuf(att, "sqT", [P, 3, NTOK])
                        skT = sbuf(att, "skT", [P, NTOK])
                        mqT = sbuf(att, "mqT", [P, MH, NTOK])
                        mkT = sbuf(att, "mkT", [P, MH, NTOK])
                        mv = sbuf(att, "mv", [P, NT, MH, HD])
                        phase_attention_features(l, patt, sqT, skT, mqT, mkT, mv)
                        cat = sbuf(att, "cat", [P, nq, D])
                        phase_attention(l, nq, patt, sqT, skT, mqT, mkT, mv, cat)
                    U = sbuf(keep, "U", [P, NT, 2, GH * HD])
                    WT = sbuf(keep, "WT", [P, NT, 2, 3 * P])
                    QT = sbuf(keep, "QT", [P, NT, 2, 3 * P])
                    IT = sbuf(keep, "IT", [P, NT, 2, GH * CHUNK])
                    KO = sbuf(keep, "KO", [P, NT, 2, GH * HD])
                    gS = sbuf(keep, "gS", [P, NT, 2, 2, 3])
                    phase_gdn_prepare(l, zb, feat, gqT, gkT, U, WT, QT, IT, KO, gS)
                phase_gdn_scan(l, nq, U, WT, QT, IT, KO, gS, ob)
                


        def run_all():
            phase_modulation()
            for l in range(NLAYER):
                nq = NT if l < NLAYER - 1 else NLT
                moe = ExitStack()
                with ExitStack() as st:
                    zb = sbuf(st, "zb", [P, NT, W_ZB])
                    ob = sbuf(st, "ob", [P, NT, GH * HD])
                    mixer(l, nq, zb, ob)
                    score = sbuf(moe, "score", [P, nq, NE])
                    phase_merge(l, nq, zb, ob, score)
                with moe:
                    dest = sbuf(moe, "dest", [P, nq, TOPK], I32)
                    wk = sbuf(moe, "wk", [P, nq, TOPK])
                    idx = sbuf(moe, "idx", [P, NBMAX + 2], I32)
                    bexp = sbuf(moe, "bexp", [1, NBMAX + 4], I32)
                    phase_route(l, nq, score, dest, wk, idx, bexp)

                    phase_experts(l, nq, idx, bexp)
                    phase_combine(l, nq, dest, wk)

        run_all()


_OUT = ((1, SEQ, D), "float32")


def kernel(**inputs):
    import numpy as _np
    import concourse.bacc as _bacc
    from concourse import mybir as _mybir
    from concourse.bass_utils import run_bass_kernel_spmd as _run

    I = {k: _np.asarray(v) for k, v in inputs.items()}
    L = NLAYER
    cols = lambda v: v.reshape(L, -1, P).transpose(0, 2, 1)
    rows = lambda v: _np.broadcast_to(v.reshape(L, 1, -1), (L, P, v.reshape(L, -1).shape[1]))
    pieces = lambda w: _np.ascontiguousarray(w.reshape(L, -1, P, w.shape[-1]).transpose(0, 2, 1, 3))
    conv = I["gdn_conv_w"].reshape(L, CONV, NGT, P).transpose(0, 3, 2, 1).reshape(L, P, NGT * CONV)
    small = _np.concatenate([cols(I["mix_norm_pre"]), cols(I["mix_norm_post"]), cols(I["ffn_norm_pre"]),
                             cols(I["ffn_norm_post"]), cols(I["ada_b"]), conv,
                             rows(I["swa_sink"]), rows(I["gdn_a_log"]), rows(I["gdn_dt_bias"]), rows(I["gdn_norm_w"]),
                             rows(I["mla_q_norm"]), rows(I["mla_kv_norm"]), rows(I["router_bias"])], axis=2)
    w = I["w_in"]
    g0, g1 = O_CQ, O_CQ + GCH
    z0 = g1 + W_ZB
    gate = _np.concatenate([I["expert_w_gate"], I["shared_w_gate"][:, None]], 1)
    up = _np.concatenate([I["expert_w_up"], I["shared_w_up"][:, None]], 1)
    down = _np.concatenate([I["expert_w_down"], I["shared_w_down"][:, None]], 1)
    split = lambda a: a.reshape(L * (NE + 1), -1, P, a.shape[-1]).transpose(0, 2, 1, 3)
    uq = I["mla_w_uq"]
    arrays = {
        "x": I["x"].reshape(SEQ, D), "ctx": I["ctx"].reshape(CTXN, D),
        "cond": _np.stack([I["c"].reshape(DK, P).T, I["c_ctx"].reshape(DK, P).T], 2),
        "ada": I["ada_w"].reshape(L, DK, P, 12, 512).transpose(0, 3, 2, 1, 4).reshape(L * 12, P, DK, 512),
        "small": small, "const": shape_constants()[0],
        "w_tok": pieces(_np.concatenate([w[..., :g0], w[..., z0:], w[..., g1:z0]], -1)),
        "w_gdn": pieces(w[..., g0:g1]),
        "w_out": pieces(I["w_out"]),
        "w_uq": uq, "w_ukv": I["mla_w_ukv"], "router": pieces(I["router_w"]),
        "w_gu": _np.concatenate([split(gate), split(up)], 3),
        "w_dn": split(down),
    }
    arrays = {k: _np.ascontiguousarray(v) for k, v in arrays.items()}
    nc = _bacc.Bacc("TRN2", target_bir_lowering=False, num_devices=1)
    aps = {k: nc.dram_tensor("in_" + k, v.shape, _mybir.dt.from_np(v.dtype), kind="ExternalInput").ap()
           for k, v in arrays.items()}
    out = nc.dram_tensor("out_x", _OUT[0], _mybir.dt.from_np(_np.dtype(_OUT[1])), kind="ExternalOutput").ap()
    build(nc, aps, out)
    r = _run(nc, [{"in_" + k: v for k, v in arrays.items()}], core_ids=[0])
    return r.results[0]["out_x"]
```
